# Optimizing a Trainium2 kernel written in Bass

```python
import math
import jax, jax.numpy as jnp
from jax import lax
import numpy as np

D_MODEL = 1024
BATCH = 1
SEQ = 512
DEPTH = 2
DEC_BATCH = 8
DEC_SEQ = 16
PAST_LEN = 512

CHUNK = 64
Q_BLOCK = 128
N_A_LAYERS = max(1, DEPTH // 2)
N_B_LAYERS = DEPTH - N_A_LAYERS
HD_A = 64
H_A = D_MODEL // (2 * HD_A)
QA = H_A * 2 * HD_A
HD_B = 64
H_B = D_MODEL // HD_B
QB = H_B * HD_B
ROT_DIM = HD_A // 4
ROPE_THETA = 500000.0
D_FF = 2816
RMS_EPS = 1e-6
FORGET_BIAS_INIT = 2.0

kernel_name = 'yoco_diff_fox_macaron_stream_step'

def rms_norm(x, g):
    xf = x.astype(jnp.float32)
    y = xf * lax.rsqrt(jnp.mean(xf * xf, axis=-1, keepdims=True) + RMS_EPS)
    return (y * g.astype(jnp.float32)).astype(x.dtype)

def swiglu(x, w_gate, w_up, w_down):
    return (jax.nn.silu(x @ w_gate) * (x @ w_up)) @ w_down

def partial_rope(x, pos):
    half = ROT_DIM // 2
    inv_freq = jnp.power(ROPE_THETA, -jnp.arange(half, dtype=jnp.float32) * 2.0 / ROT_DIM)
    ang = pos[:, None] * inv_freq[None, :]
    shape = (pos.shape[0],) + (1,) * (x.ndim - 3) + (half,)
    cos = jnp.cos(ang).reshape(shape).astype(x.dtype)
    sin = jnp.sin(ang).reshape(shape).astype(x.dtype)
    x1 = x[..., :half]
    x2 = x[..., half:ROT_DIM]
    return jnp.concatenate([x1 * cos - x2 * sin, x2 * cos + x1 * sin, x[..., ROT_DIM:]], axis=-1)

def to_blocks(a):
    b, t = a.shape[:2]
    a = a.reshape((b, t // Q_BLOCK, Q_BLOCK) + a.shape[2:])
    return jnp.moveaxis(a, 1, 0)

def from_blocks(a):
    a = jnp.moveaxis(a, 0, 1)
    return a.reshape((a.shape[0], a.shape[1] * a.shape[2]) + a.shape[3:])

def diff_attn_prompt(q, k, v, lam):
    t = q.shape[1]
    scale = HD_A ** -0.5
    key_chunk = jnp.arange(t) // CHUNK

    def block(args):
        qb, bi = args
        qpos = bi * Q_BLOCK + jnp.arange(Q_BLOCK)
        mask = key_chunk[None, :] <= (qpos // CHUNK)[:, None]
        s = jnp.einsum('bqhcd,bkhcd->bhcqk', qb, k, preferred_element_type=jnp.float32) * scale
        p = jax.nn.softmax(jnp.where(mask, s, -jnp.inf), axis=-1)
        pd = p[:, :, 0] - lam * p[:, :, 1]
        return jnp.einsum('bhqk,bkhe->bqhe', pd.astype(v.dtype), v)

    out = lax.map(block, (to_blocks(q), jnp.arange(t // Q_BLOCK)))
    return from_blocks(out)

def diff_attn_sample(q, k_new, v_new, k_past, v_past, lam):
    p_len = k_past.shape[1]
    scale = HD_A ** -0.5
    s = jnp.concatenate([
        jnp.einsum('bqhcd,bkhcd->bhcqk', q, k_past, preferred_element_type=jnp.float32),
        jnp.einsum('bqhcd,bkhcd->bhcqk', q, k_new, preferred_element_type=jnp.float32)], axis=-1) * scale
    p = jax.nn.softmax(s, axis=-1)
    pd = (p[:, :, 0] - lam * p[:, :, 1]).astype(v_new.dtype)
    return (jnp.einsum('bhqk,bkhe->bqhe', pd[..., :p_len], v_past)
            + jnp.einsum('bhqk,bkhe->bqhe', pd[..., p_len:], v_new))

def fox_prompt(q, k, v, logf):
    t = q.shape[1]
    scale = HD_B ** -0.5
    f_cum = jnp.cumsum(logf, axis=1)
    f_key = jnp.transpose(f_cum, (0, 2, 1))
    kpos = jnp.arange(t)

    def block(args):
        qb, fq, bi = args
        qpos = bi * Q_BLOCK + jnp.arange(Q_BLOCK)
        s = jnp.einsum('bqhd,bkhd->bhqk', qb, k, preferred_element_type=jnp.float32) * scale
        s = s + jnp.transpose(fq, (0, 2, 1))[..., None] - f_key[:, :, None, :]
        s = jnp.where(kpos[None, :] <= qpos[:, None], s, -jnp.inf)
        p = jax.nn.softmax(s, axis=-1)
        return jnp.einsum('bhqk,bkhd->bqhd', p.astype(v.dtype), v)

    out = lax.map(block, (to_blocks(q), to_blocks(f_cum), jnp.arange(t // Q_BLOCK)))
    return from_blocks(out)

def fox_sample(q, k_new, v_new, logf_new, k_past, v_past, logf_past):
    p_len = k_past.shape[1]
    t = q.shape[1]
    scale = HD_B ** -0.5
    f_cum = jnp.cumsum(jnp.concatenate([logf_past.astype(jnp.float32), logf_new], axis=1), axis=1)
    f_bht = jnp.transpose(f_cum, (0, 2, 1))
    f_q = f_bht[:, :, p_len:]
    s_past = (jnp.einsum('bqhd,bkhd->bhqk', q, k_past, preferred_element_type=jnp.float32) * scale
              + f_q[..., None] - f_bht[:, :, None, :p_len])
    s_new = (jnp.einsum('bqhd,bkhd->bhqk', q, k_new, preferred_element_type=jnp.float32) * scale
             + f_q[..., None] - f_q[:, :, None, :])
    causal = jnp.tril(jnp.ones((t, t), dtype=bool))
    s_new = jnp.where(causal, s_new, -jnp.inf)
    p = jax.nn.softmax(jnp.concatenate([s_past, s_new], axis=-1), axis=-1).astype(v_new.dtype)
    return (jnp.einsum('bhqk,bkhd->bqhd', p[..., :p_len], v_past)
            + jnp.einsum('bhqk,bkhd->bqhd', p[..., p_len:], v_new))

def trunk(x, past, g_norm, w_ffn_gate, w_ffn_up, w_ffn_down, w_qkv_a, lambda_a, g_sub_a, w_o_a,
          g_kv_b, w_kv_b, w_f_b, b_f_b, w_q_b, w_o_b, g_final):
    b, t, _ = x.shape
    p0 = 0 if past is None else past[0].shape[2]
    pos = jnp.arange(t, dtype=jnp.float32) + p0
    a_k, a_v = [], []
    b_k = b_v = b_logf = None
    for l in range(DEPTH):
        if l == N_A_LAYERS:
            hkv = rms_norm(x, g_kv_b)
            kv = (hkv @ w_kv_b).reshape(b, t, 2, H_B, HD_B)
            b_k, b_v = kv[:, :, 0], kv[:, :, 1]
            b_logf = jax.nn.log_sigmoid((hkv @ w_f_b).astype(jnp.float32) + b_f_b.astype(jnp.float32))
        x = x + 0.5 * swiglu(rms_norm(x, g_norm[l, 0]), w_ffn_gate[l, 0], w_ffn_up[l, 0], w_ffn_down[l, 0])
        h = rms_norm(x, g_norm[l, 1])
        if l < N_A_LAYERS:
            qkv = h @ w_qkv_a[l]
            q = partial_rope(qkv[..., :QA].reshape(b, t, H_A, 2, HD_A), pos)
            k = partial_rope(qkv[..., QA:2 * QA].reshape(b, t, H_A, 2, HD_A), pos)
            v = qkv[..., 2 * QA:].reshape(b, t, H_A, 2 * HD_A)
            lam_init = 0.8 - 0.6 * math.exp(-0.3 * l)
            lq = lambda_a[l].astype(jnp.float32)
            lam = jnp.exp(jnp.sum(lq[0] * lq[1])) - jnp.exp(jnp.sum(lq[2] * lq[3])) + lam_init
            if past is None:
                o = diff_attn_prompt(q, k, v, lam)
            else:
                o = diff_attn_sample(q, k, v, past[0][l], past[1][l], lam)
            o = rms_norm(o, g_sub_a[l]) * (1.0 - lam_init)
            x = x + o.reshape(b, t, QA) @ w_o_a[l]
            a_k.append(k)
            a_v.append(v)
        else:
            j = l - N_A_LAYERS
            q = (h @ w_q_b[j]).reshape(b, t, H_B, HD_B)
            if past is None:
                o = fox_prompt(q, b_k, b_v, b_logf)
            else:
                o = fox_sample(q, b_k, b_v, b_logf, past[2], past[3], past[4])
            x = x + o.reshape(b, t, QB) @ w_o_b[j]
        x = x + 0.5 * swiglu(rms_norm(x, g_norm[l, 2]), w_ffn_gate[l, 1], w_ffn_up[l, 1], w_ffn_down[l, 1])
    y = rms_norm(x, g_final)
    return y, jnp.stack(a_k), jnp.stack(a_v), b_k, b_v, b_logf

def setup_inputs(seed: int = 0) -> dict:
    key = jax.random.key(seed)
    ks = jax.random.split(key, 22)
    D = D_MODEL

    def nrm(k, shape, scale):
        return scale * jax.random.normal(k, shape, dtype=jnp.float32)

    return {
        'x_prompt': nrm(ks[0], (BATCH, SEQ, D), 1.0),
        'x_sample': nrm(ks[1], (DEC_BATCH, DEC_SEQ, D), 1.0),
        'cache_a_k': nrm(ks[2], (N_A_LAYERS, DEC_BATCH, PAST_LEN, H_A, 2, HD_A), 1.0),
        'cache_a_v': nrm(ks[3], (N_A_LAYERS, DEC_BATCH, PAST_LEN, H_A, 2 * HD_A), 1.0),
        'cache_b_k': nrm(ks[4], (DEC_BATCH, PAST_LEN, H_B, HD_B), 1.0),
        'cache_b_v': nrm(ks[5], (DEC_BATCH, PAST_LEN, H_B, HD_B), 1.0),
        'cache_b_logf': jax.nn.log_sigmoid(FORGET_BIAS_INIT + nrm(ks[6], (DEC_BATCH, PAST_LEN, H_B), 1.0)),
        'g_norm': 1.0 + nrm(ks[7], (DEPTH, 3, D), 0.02),
        'w_ffn_gate': nrm(ks[8], (DEPTH, 2, D, D_FF), D ** -0.5),
        'w_ffn_up': nrm(ks[9], (DEPTH, 2, D, D_FF), D ** -0.5),
        'w_ffn_down': nrm(ks[10], (DEPTH, 2, D_FF, D), D_FF ** -0.5),
        'w_qkv_a': nrm(ks[11], (N_A_LAYERS, D, 3 * QA), D ** -0.5),
        'lambda_a': nrm(ks[12], (N_A_LAYERS, 4, HD_A), 0.1),
        'g_sub_a': 1.0 + nrm(ks[13], (N_A_LAYERS, 2 * HD_A), 0.02),
        'w_o_a': nrm(ks[14], (N_A_LAYERS, QA, D), QA ** -0.5),
        'g_kv_b': 1.0 + nrm(ks[15], (D,), 0.02),
        'w_kv_b': nrm(ks[16], (D, 2 * QB), D ** -0.5),
        'w_f_b': nrm(ks[17], (D, H_B), D ** -0.5),
        'b_f_b': FORGET_BIAS_INIT + nrm(ks[18], (H_B,), 0.1),
        'w_q_b': nrm(ks[19], (N_B_LAYERS, D, QB), D ** -0.5),
        'w_o_b': nrm(ks[20], (N_B_LAYERS, QB, D), QB ** -0.5),
        'g_final': 1.0 + nrm(ks[21], (D,), 0.02),
    }

def reference(x_prompt, x_sample, cache_a_k, cache_a_v, cache_b_k, cache_b_v, cache_b_logf,
              g_norm, w_ffn_gate, w_ffn_up, w_ffn_down, w_qkv_a, lambda_a, g_sub_a, w_o_a,
              g_kv_b, w_kv_b, w_f_b, b_f_b, w_q_b, w_o_b, g_final):
    y_prompt, new_a_k_prompt, new_a_v_prompt, new_b_k_prompt, new_b_v_prompt, new_b_logf_prompt = trunk(
        x_prompt, None, g_norm, w_ffn_gate, w_ffn_up, w_ffn_down, w_qkv_a, lambda_a, g_sub_a, w_o_a,
        g_kv_b, w_kv_b, w_f_b, b_f_b, w_q_b, w_o_b, g_final)
    y_sample, new_a_k_sample, new_a_v_sample, new_b_k_sample, new_b_v_sample, new_b_logf_sample = trunk(
        x_sample, (cache_a_k, cache_a_v, cache_b_k, cache_b_v, cache_b_logf),
        g_norm, w_ffn_gate, w_ffn_up, w_ffn_down, w_qkv_a, lambda_a, g_sub_a, w_o_a,
        g_kv_b, w_kv_b, w_f_b, b_f_b, w_q_b, w_o_b, g_final)
    return (y_prompt, y_sample,
            new_a_k_prompt, new_a_v_prompt, new_b_k_prompt, new_b_v_prompt, new_b_logf_prompt,
            new_a_k_sample, new_a_v_sample, new_b_k_sample, new_b_v_sample, new_b_logf_sample)


_drawn_inputs = setup_inputs


def setup_inputs(seed=0):
    import zlib

    import numpy as np

    out = dict(_drawn_inputs(seed))
    spreads = {}
    factors = {'g_sub_a': 4.038,
     'g_kv_b': 7.941,
     'g_final': 20.743,
     'cache_b_logf': 8.188,
     'b_f_b': 3.409}
    for name, (base, spread) in spreads.items():
        noise = np.random.default_rng([zlib.crc32(name.encode()), seed]).standard_normal(out[name].shape)
        drawn = base * np.exp(spread * noise) if base else spread * noise
        out[name] = __import__('jax').numpy.asarray(drawn.astype(out[name].dtype))
    for name, factor in factors.items():
        out[name] = (out[name] * factor).astype(out[name].dtype)
    return out
```

```python
from contextlib import ExitStack, contextmanager

import concourse.bass as bass
from concourse import mybir

F32 = mybir.dt.float32
F32R = mybir.dt.float32r
ALU = mybir.AluOpType
ACT = mybir.ActivationFunctionType
AX = mybir.AxisListType.X

P = 128
D = 1024
KB = D // P
NP, DB, DS = 512, 8, 16
T = NP + DB * DS
TB = T // P
HT = T // 2
FF = 2816
GRP = 2
FB = FF // P // GRP
PAST = 512
PB = PAST // P
PAIR = 8
HB = 16
EPS = 1e-6
SCALE = 0.125
NEG = -1e30
LAM_INIT = 0.2

IDENT, CAUSAL, CHUNKED, SPREAD, SAME, OTHER, STEP, QSEL, QTRI = (i * P for i in range(9))
COMP0 = 9 * P
COMP1 = COMP0 + 1
ROPE = COMP0 + 2
NCONST = ROPE + TB * 16

FFN_TILES = GRP * (2 * FB + KB)
QKV_TILES, KV_TILES, SQ_TILES = 24, 16, 8
BASE = {}
_n = 0
for _name, _k in (("ffn0", FFN_TILES), ("qkv", QKV_TILES), ("oa", SQ_TILES), ("ffn1", FFN_TILES), ("kv", KV_TILES),
                  ("wf", 1), ("ffn2", FFN_TILES), ("qb", SQ_TILES), ("ob", SQ_TILES), ("ffn3", FFN_TILES)):
    BASE[_name] = _n
    _n += _k


def primed(n):
    return n + 1


class Count:

    def __init__(self):
        self.n, self.off = 0, 0

    def next(self):
        self.n += 1
        return self.off + self.n

    @contextmanager
    def loop(self, i, trips, per):
        n, off = self.n, self.off
        self.off = off + i * per
        yield
        assert self.n - n == per, (self.n - n, per)
        self.n, self.off = n + trips * per, off


def yoco_stream_step(nc, x_prompt, x_sample, cache_a_k, cache_a_v, cache_b_k, cache_b_v, cache_b_logf,
                     g_norm, w_ffn_gate, w_ffn_up, w_ffn_down, w_qkv_a, lambda_a, g_sub_a, w_o_a,
                     g_kv_b, w_kv_b, w_f_b, b_f_b, w_q_b, w_o_b, g_final, shape_consts, new_mask,
                     y_prompt, y_sample, ak_prompt, av_prompt, bk_prompt, bv_prompt, bf_prompt,
                     ak_sample, av_sample, bk_sample, bv_sample, bf_sample, f_prompt_scr, f_sample_scr):
    with ExitStack() as ctx:
        ctx.enter_context(nc.allow_non_contiguous_dma("gate biases and log-forget rows"))

        def sb(name, shape, dt=F32):
            return ctx.enter_context(nc.sbuf_tensor(name, shape, dt))

        def lent(*specs):
            with ExitStack() as s:
                return [s.enter_context(nc.sbuf_tensor(*spec)) for spec in specs]

        sems = {}

        def sem(name):
            if name not in sems:
                sems[name] = ctx.enter_context(nc.semaphore(name))
            return sems[name]

        xT = sb("xT", [P, KB, T])
        xn_hi, xn_lo = lent(("xn_hi", [P, KB, T], F32R), ("xn_lo", [P, KB, T], F32R))
        qT = sb("qT", [P, PAIR, T])
        oT = sb("oT", [P, PAIR, T])
        act_hi, act_lo = lent(("act_hi", [P, FB, T], F32R), ("act_lo", [P, FB, T], F32R))
        R1 = sb("R1", [P, 2 * FB * T])
        kT = sb("kT", [P, PAIR, T])
        vN = sb("vN", [P, TB, D])
        raw = [sb(f"raw{i}", [P, FB * P]) for i in range(2)]
        w_hi = [sb(f"w_hi{i}", [P, FB * P], F32R) for i in range(2)]
        w_lo = [sb(f"w_lo{i}", [P, FB * P], F32R) for i in range(2)]
        cst = sb("cst", [P, NCONST])
        gT = sb("gT", [P, 68])
        t0 = sb("t0", [P, T])
        t1 = sb("t1", [P, T])
        t2 = sb("t2", [P, T])
        sqacc = sb("sqacc", [P, T])
        ones_d = sb("ones_d", [P, P])
        ones_e = sb("ones_e", [P, P])
        Cm = sb("Cm", [P, 2, P])
        st = sb("st", [P, 2, 8])
        small = sb("small", [P, 32])
        PS = ctx.enter_context(nc.psum_tensor("PS", [P, 8, 512], F32))

        ident = cst[:, IDENT:IDENT + P]
        nat = R1[:, 0:2 * TB * D].rearrange("p (w t c) -> p w t c", w=2, t=TB)
        Knat = R1[:, 0:4096].rearrange("p (k c) -> p k c", k=PB)
        kTc = R1[:, 4096:8192].rearrange("p (h k) -> p h k", h=PAIR)
        Vc = R1[:, 8192:12288].rearrange("p (k c) -> p k c", k=PB)
        qbd = R1[:, 12288:12544].rearrange("p (h m) -> p h m", h=PAIR)
        oN = R1[:, 12544:12800].rearrange("p (g m) -> p g m", g=2)
        FS = R1[:, 12800:14080].rearrange("p (g m) -> p g m", g=2)
        PR = R1[:, 4096:6144].rearrange("p (r c k) -> p r c k", r=2, c=2)
        pT = R1[:, 6144:10240].rearrange("p (c k q) -> p c k q", c=2, k=PB)
        FP = R1[:, 10240:11264].rearrange("p (c k) -> p c k", c=2)
        qh = R1[:, 11264:11776]
        kh = R1[:, 12288:12800]
        vh = R1[:, 11776:12288].rearrange("p (k e) -> p k e", k=PB)
        xN = R1[:, 0:TB * D].rearrange("p (t c) -> p t c", t=TB)
        yT = R1[:, 0:KB * T].rearrange("p (k t) -> p k t", k=KB)
        yN = R1[:, KB * T:2 * KB * T].rearrange("p (t c) -> p t c", t=TB)
        gN = R1[:, 13312:13440]
        lamN = R1[:, 13440:13696]
        own = R1[0:1, 12800:13824]
        qraw = R1[:, 0:PAIR * T].rearrange("p (h t) -> p h t", h=PAIR)
        LN = R1[:, 5120:5632].rearrange("p (k m) -> p k m", k=PB)
        LT = R1[:, 5632:6144]
        lfT = R1[0:HB, 6144:6784]
        lf1 = R1[0:HB, 6784:7424]
        lf2 = R1[0:HB, 7424:8064]
        FCp = R1[0:HB, 8064:8576]
        lfN = R1[:, 8576:8656].rearrange("p (t h) -> p t h", t=TB)
        EX = R1[:, 8704:8832]
        FC = R1[:, 8832:9360]
        LO = R1[:, 9408:10048]
        rope_consts = cst[:, ROPE:ROPE + TB * 16].rearrange("p (t c) -> p t c", t=TB)

        def pair(n):
            return PS[:, 2 * n:2 * n + 2, 0:HT]

        def halves(ap):
            return ap.rearrange("p (b n) -> p b n", b=2)

        def wide(bank, n=T):
            return PS[:, bank:bank + 2, :].rearrange("p b n -> p (b n)")[:, 0:n]

        def gcol(j, k=None):
            return gT[:, 8 * j:8 * j + 8] if k is None else gT[:, 8 * j + k:8 * j + k + 1]

        GSUB = gT[:, 64:65]
        neg_lam, comp = small[:, 0:1], small[:, 1:2]
        gsub = small[:, 2:3]
        G_KV, G_FINAL = 6, 7

        w_loaded = [sem("w_loaded0"), sem("w_loaded1")]
        w_hi_made, w_split, w_used = sem("w_hi_made"), sem("w_split"), sem("w_used")
        setup_in, stored = sem("setup_in"), sem("stored")
        stores = [0]

        block = ctx.enter_context(nc.Block())

        @block.sync
        def _(sp):
            sp.dma_start(xN[:, 0:4, :], x_prompt[0].rearrange("(t p) d -> p t d", p=P)).then_inc(setup_in, 16)
            sp.dma_start(xN[:, 4, :], x_sample.rearrange("b t d -> (b t) d")).then_inc(setup_in, 16)
            sp.dma_start(cst[:, :], shape_consts).then_inc(setup_in, 16)
            sp.dma_start(gN[0:48, :], g_norm.rearrange("l j (k p) -> (l j k) p", p=P)).then_inc(setup_in, 16)
            sp.dma_start(gN[48:56, :], g_kv_b.rearrange("(k p) -> k p", p=P)).then_inc(setup_in, 16)
            sp.dma_start(gN[56:64, :], g_final.rearrange("(k p) -> k p", p=P)).then_inc(setup_in, 16)
            sp.dma_start(gN[64:65, :], g_sub_a).then_inc(setup_in, 16)
            sp.dma_start(lamN[:, :], lambda_a.rearrange("l c d -> l (c d)").to_broadcast([P, 4 * 64])).then_inc(setup_in, 16)
            sp.dma_start(small[0:HB, 3:4], b_f_b.rearrange("(h o) -> h o", o=1)).then_inc(setup_in, 16)

            def tile(n, slot, view, src):
                if not isinstance(n, int) or n >= 2:
                    sp.wait_ge(w_split, n - 1)
                sp.dma_start(view, src).then_inc(w_loaded[slot], 16)

            def cols(w, slot, at, kb=KB):
                return (raw[slot][:, 0:kb * P].rearrange("p (k m) -> p k m", k=kb),
                        w[:, bass.ds(at, P)].rearrange("(k p) m -> p k m", p=P))

            def load_ffn(f, base):
                l, j = f // 2, f % 2
                gate, up, down = w_ffn_gate[l, j], w_ffn_up[l, j], w_ffn_down[l, j]
                for g in range(GRP):
                    at = base + g * (2 * FB + KB)
                    first = 0
                    if at == 0:
                        tile(0, 0, *cols(gate, 0, 0))
                        tile(1, 1, *cols(up, 1, 0))
                        first = 1
                    with sp.Fori(first, FB) as i:
                        s = at % 2
                        tile(at + i * 2, s, *cols(gate, s, (i + g * FB) * P))
                        tile(at + i * 2 + 1, 1 - s, *cols(up, 1 - s, (i + g * FB) * P))
                    at += 2 * FB
                    rows = down[g * FB * P:(g + 1) * FB * P, :]
                    with sp.Fori(0, KB // 2) as m:
                        s = at % 2
                        tile(at + m * 2, s, *cols(rows, s, m * 2 * P, FB))
                        tile(at + m * 2 + 1, 1 - s, *cols(rows, 1 - s, m * 2 * P + P, FB))

            def load_square(w, base):
                with sp.Fori(0, KB // 2) as m:
                    s = base % 2
                    tile(base + m * 2, s, *cols(w, s, m * 2 * P))
                    tile(base + m * 2 + 1, 1 - s, *cols(w, 1 - s, m * 2 * P + P))

            def load_rows(w, base, n_tiles):
                with sp.Fori(0, n_tiles) as n:
                    for u in range(4):
                        s = (base + u) % 2
                        tile(base + n * 4 + u, s, raw[s][:, 0:1024].rearrange("p (k m) -> p k m", k=2),
                             w[u * 256:(u + 1) * 256, bass.ds(n * 512, 512)].rearrange("(k p) m -> p k m", p=P))

            def load_cache(x, kc, vc, f_scr):
                if x == "A":
                    sp.wait_ge(sem("ht_readyA"), 32)
                    sp.dma_start(own, new_mask).then_inc(sem("own_in"), 16)
                else:
                    sp.wait_ge(sem("qT_copied"), 1)

                def keys(b):
                    sp.dma_start(Knat, kc[b].rearrange("(k p) c -> p k c", p=P)).then_inc(sem("k_in" + x), 16)

                def values(b):
                    sp.dma_start(Vc, vc[b].rearrange("(k p) c -> p k c", p=P)).then_inc(sem("v_in" + x), 16)

                def forget(b):
                    if f_scr is not None:
                        for hg in range(2):
                            src = f_scr[bass.ds(b * HB + hg * 8, 8), :].rearrange("h (o n) -> h o n", o=1)
                            sp.dma_start(FS[:, hg, :], src.to_broadcast([8, DS, T])).then_inc(sem("f_in" + x), 16)

                keys(0)
                sp.wait_ge(sem("o_ready" + x), primed(PAIR))
                values(0)
                forget(0)
                with sp.Fori(1, DB) as b:
                    sp.wait_ge(sem("kt_ready" + x), b * 8)
                    keys(b)
                    if f_scr is not None:
                        sp.wait_ge(sem("biased" + x), b * 2)
                        forget(b)
                    sp.wait_ge(sem("pv_ready" + x), b * 2)
                    values(b)

            load_ffn(0, BASE["ffn0"])
            load_rows(w_qkv_a[0], BASE["qkv"], 6)
            load_cache("A", cache_a_k[0].rearrange("b t h c d -> b t (h c d)"),
                       cache_a_v[0].rearrange("b t h e -> b t (h e)"), None)
            load_square(w_o_a[0], BASE["oa"])
            load_ffn(1, BASE["ffn1"])
            load_rows(w_kv_b, BASE["kv"], 4)
            s = BASE["wf"] % 2
            tile(BASE["wf"], s, raw[s][:, 0:1024].rearrange("p (k m) -> p k m", k=KB)[:, :, 0:HB],
                 w_f_b.rearrange("(k p) h -> p k h", p=P))
            sp.wait_ge(w_used, BASE["kv"])
            for k in range(PB):
                sp.dma_start(LN[:, k, :].rearrange("p (b h) -> p b h", b=DB),
                             cache_b_logf[:, k * P:(k + 1) * P, :].rearrange("b p h -> p b h")).then_inc(sem("logf_in"), 16)
            load_ffn(2, BASE["ffn2"])
            load_square(w_q_b[0], BASE["qb"])
            with sp.Fori(0, PAIR) as p:
                sp.wait_ge(sem("rows_free"), p + 1)
                for c in range(2):
                    sp.dma_start(FP[:, c, :], f_prompt_scr[bass.ds(p * 2 + c, 1), :].to_broadcast([P, NP])).then_inc(
                        sem("row_in"), 16)
            load_cache("B", cache_b_k.rearrange("b t h d -> b t (h d)"), cache_b_v.rearrange("b t h d -> b t (h d)"),
                       f_sample_scr)
            load_square(w_o_b[0], BASE["ob"])
            load_ffn(3, BASE["ffn3"])

        @block.gpsimd
        def _(pool):
            def split(n, slot, words, landed):
                pool.wait_ge(w_loaded[slot], landed)
                if not isinstance(n, int) or n >= 2:
                    pool.wait_ge(w_used, n - 1)
                pool.sem_inc(sem("pool_passed"), 1)
                pool.tensor_copy(w_hi[slot][:, 0:words], raw[slot][:, 0:words]).then_inc(w_hi_made, 1)
                pool.wait_ge(w_hi_made, n + 1)
                pool.tensor_tensor(w_lo[slot][:, 0:words], raw[slot][:, 0:words],
                                   w_hi[slot][:, 0:words].bitcast(F32), ALU.subtract).then_inc(w_split, 1)

            def run(base, count, words):
                first = 0
                if base == 0:
                    split(0, 0, words, 16)
                    split(1, 1, words, 16)
                    first = 1
                with pool.Fori(first, count // 2) as i:
                    for u in range(2):
                        s = (base + u) % 2
                        split(base + i * 2 + u, s, words, i * 16 + 16 * ((base + u) // 2 + 1))

            def run_ffn(base):
                for g in range(GRP):
                    run(base, 2 * FB, KB * P)
                    run(base + 2 * FB, KB, FB * P)
                    base += 2 * FB + KB

            run_ffn(BASE["ffn0"])
            run(BASE["qkv"], QKV_TILES, 1024)
            run(BASE["oa"], SQ_TILES, 1024)
            run_ffn(BASE["ffn1"])
            run(BASE["kv"], KV_TILES, 1024)
            n = BASE["wf"]
            split(n, n % 2, 1024, 16 * (n // 2 + 1))
            run_ffn(BASE["ffn2"])
            run(BASE["qb"], SQ_TILES, 1024)
            run(BASE["ob"], SQ_TILES, 1024)
            run_ffn(BASE["ffn3"])

        @block.tensor
        def _(pe):
            def flip(dst, src, rows=P):
                return pe.transpose(dst, src, cst[0:rows, IDENT:IDENT + rows])

            def stationary_tile(slot, kb, x_hi, x_lo, out, ready=None):
                for k in range(kb):
                    if ready is not None and ready(k) is not None:
                        pe.wait_ge(*ready(k))
                    w = slice(k * P, (k + 1) * P)
                    for a, x in ((w_hi, x_hi), (w_hi, x_lo), (w_lo, x_hi)):
                        for h in range(2):
                            last = pe.matmul(out[:, h, :], a[slot][:, w], x[:, k, h * HT:(h + 1) * HT],
                                             start=(k == 0 and a is w_hi and x is x_hi),
                                             stop=(k == kb - 1 and a is w_lo))
                last.then_inc(w_used, 1)
                return last

            def stats(n):
                pe.wait_ge(sem("squares_summed"), n + 1)
                for h in range(2):
                    last = pe.matmul(pair(0)[:, h, :], ones_d[:, :], sqacc[:, h * HT:(h + 1) * HT], start=True, stop=True)
                last.then_inc(sem("mean_ready"), 1)

            def ffn(f, base, norm):
                for g in range(GRP):
                    at = base + g * (2 * FB + KB)

                    def hidden(i, first, count):
                        s = at % 2
                        blk = count + i
                        pe.wait_ge(w_split, at + i * 2 + 1)
                        if not isinstance(blk, int) or blk >= 1:
                            pe.wait_ge(sem("gate_read"), blk)
                        stationary_tile(s, KB, xn_hi, xn_lo, pair(0),
                                        (lambda k: (sem("xn_ready"), primed(norm * KB + k + 1))) if first else None)
                        pe.wait_ge(w_split, at + i * 2 + 2)
                        if not isinstance(blk, int) or blk >= 1:
                            pe.wait_ge(sem("up_read"), primed(blk))
                        stationary_tile(1 - s, KB, xn_hi, xn_lo, pair(1))

                    count = (f * GRP + g) * FB
                    hidden(0, g == 0, count)
                    with pe.Fori(1, FB) as i:
                        hidden(i, False, count)
                    at += 2 * FB
                    ready = (f * GRP + g) * FB
                    pe.wait_ge(sem("act_ready"), primed(ready + FB - 2))
                    down(at, FB, act_hi, act_lo, lambda k: (sem("act_ready"), primed(ready + FB)) if k == FB - 2 else None)

            rounds = [0]

            def down(at, kb, hi, lo, ready=None):
                done = rounds[0] * KB
                rounds[0] += 1
                with pe.Fori(0, KB // 2) as m:
                    for u in range(2):
                        pe.wait_ge(w_split, at + m * 2 + u + 1)
                        pe.wait_ge(sem("down_read"), done + m * 2 + u + 1)
                        stationary_tile((at + u) % 2, kb, hi, lo, pair(2 + u), ready)

            def token_tile(at, done, n):
                for u in range(4):
                    s = (at + u) % 2
                    pe.wait_ge(w_split, n * 4 + (at + u + 1))
                    for kk in range(2):
                        k = 2 * u + kk
                        for t in range(TB):
                            if k == 0:
                                pe.wait_ge(sem("rows_read"), n * TB + (done * TB + t + 1))
                            cols = slice(t * P, (t + 1) * P)
                            w = slice(kk * 512, (kk + 1) * 512)
                            for x, a in ((xn_hi, w_hi), (xn_hi, w_lo), (xn_lo, w_hi)):
                                last = pe.matmul(PS[:, t, :], x[:, k, cols], a[s][:, w],
                                                 start=(k == 0 and x is xn_hi and a is w_hi), stop=(k == KB - 1 and x is xn_lo))
                    last.then_inc(w_used, 1)

            def head_transposes(x, src, parts, dsts_free):
                for w in range(parts):
                    for h in range(PAIR):
                        for g, blocks in enumerate((range(0, 4), range(4, 5))):
                            n = (w * PAIR + h) * 2 + g
                            bank = n % 4
                            if n >= 4:
                                pe.wait_ge(sem(("ht_act" if n % 2 else "ht_dve") + x), (n - 4) // 2 + 1)
                            for j, t in enumerate(blocks):
                                last = flip(PS[:, bank, j * P:(j + 1) * P], src[:, w, t, h * P:(h + 1) * P])
                            last.then_inc(sem("ht_ready" + x), 1)

            def prompt(x):
                mask = cst[:, CHUNKED:CHUNKED + P] if x == "A" else cst[:, CAUSAL:CAUSAL + P]
                s_ready, p_ready, pt_read = sem("s_ready" + x), sem("p_ready" + x), sem("pt_read" + x)
                with pe.Fori(0, PAIR) as h:
                    def scores(t):
                        if t == 0:
                            pe.wait_ge(sem("staged" + x), h + 1)
                        if t >= 2:
                            pe.wait_ge(sem("exp_doneA" if x == "A" else "nb_readyB"), h * 4 + t - 1)
                        for c in range(2):
                            rows = slice(64 * c, 64 * c + 64)
                            out = PS[:, 2 * (t % 2) + c, :]
                            pe.matmul(out[:, 0:(t + 1) * P], qh[rows, t * P:(t + 1) * P], kh[rows, 0:(t + 1) * P],
                                      start=True, stop=False)
                            last = pe.matmul(out[:, t * P:(t + 1) * P], ident, mask, start=False, stop=True)
                        last.then_inc(s_ready, 1)

                    def turn(t):
                        pe.wait_ge(p_ready, h * 4 + t + 1)
                        if t >= 1:
                            pe.wait_ge(pt_read, h * 4 + t)
                        for c in range(1 if x == "A" else 2):
                            for k in range(t + 1):
                                last = flip(PS[:, 4 + c, k * P:(k + 1) * P], PR[:, t % 2, c, k * P:(k + 1) * P])
                        last.then_inc(sem("pt_ready" + x), 1)

                    scores(0)
                    scores(1)
                    turn(0)
                    scores(2)
                    turn(1)
                    scores(3)
                    turn(2)
                    turn(3)
                    pe.wait_ge(pt_read, h * 4 + 4)
                    pe.wait_ge(sem("o_read" + x), primed(h))
                    for c in range(1 if x == "A" else 2):
                        e = slice(0, P) if x == "A" else slice(64 * c, 64 * c + 64)
                        for k in range(PB):
                            last = pe.matmul(PS[e, 6, k * P:512], vh[:, k, e], pT[:, c, k, k * P:512],
                                             start=(k == 0), stop=(k == PB - 1), skip_group_check=True)
                    last.then_inc(sem("o_ready" + x), 1)

            def sample(x):
                def turn_keys(b):
                    pe.wait_ge(sem("k_in" + x), b * 16 + 16)
                    for h in range(PAIR):
                        if h >= 4:
                            pe.wait_ge(sem(("kt_dve" if h % 2 else "kt_act") + x), b * 4 + (h - 4) // 2 + 1)
                        for k in range(PB):
                            last = flip(PS[:, h % 4, k * P:(k + 1) * P], Knat[:, k, h * P:(h + 1) * P])
                        last.then_inc(sem("kt_ready" + x), 1)

                def stream(b, following):
                    pe.wait_ge(sem("kt_dve" + x), b * 4 + 4)
                    pe.wait_ge(sem("kt_act" + x), b * 4 + 4)
                    pe.wait_ge(sem("q_staged" + x), b + 1)
                    for g in range(2):
                        pe.wait_ge(sem("oT_read" + x), primed(b * 2))
                        for j in range(4):
                            h, rows = 4 * g + j, slice(32 * j, 32 * j + 32)
                            pe.matmul(PS[rows, 4 + 2 * g, :], qbd[:, h, :], kTc[:, h, :], start=True, stop=True,
                                      tile_position=(0, 32 * j), skip_group_check=True)
                            pe.matmul(PS[rows, 5 + 2 * g, 0:P], qbd[:, h, :], kT[:, h, NP:T], start=True, stop=False,
                                      tile_position=(0, 32 * j), skip_group_check=True)
                        if x == "A":
                            last = pe.matmul(PS[:, 5 + 2 * g, 0:P], ones_e[0:1, :], own[0:1, bass.ds(b * P, P)], start=False, stop=True,
                                             skip_group_check=True)
                        else:
                            last = pe.matmul(PS[:, 5 + 2 * g, 0:P], cst[0:DS, QSEL:QSEL + P], cst[0:DS, QTRI:QTRI + P],
                                             start=False, stop=True, skip_group_check=True)
                        last.then_inc(sem("ss_ready" + x), 1)
                    if following:
                        turn_keys(b + 1)
                    for g in range(2):
                        pe.wait_ge(sem("norm_ready" + x), b * 2 + g + 1)
                        if g == 0 and following:
                            pe.wait_ge(sem("kt_dve" + x), b * 4 + 8)
                            pe.wait_ge(sem("kt_act" + x), b * 4 + 8)
                        for k in range(PB + 1):
                            out = wide(2 * g)[:, k * P:(k + 1) * P]
                            last = pe.matmul(out, (t0, t1)[g][:, k * P:(k + 1) * P], Cm[:, g, :],
                                             start=True, stop=True)
                        last.then_inc(sem("pd_ready" + x), 1)
                    pe.wait_ge(sem("v_in" + x), b * 16 + 16)
                    for g in range(2):
                        pe.wait_ge(sem("pd_read" + x + str(g)), b + 1)
                        for k in range(PB + 1):
                            v = Vc[:, k, g * 512:(g + 1) * 512] if k < PB else vN[:, TB - 1, g * 512:(g + 1) * 512]
                            last = pe.matmul(PS[:, 4 + 2 * g, :], (t2, sqacc)[g][:, k * P:(k + 1) * P], v,
                                             start=(k == 0), stop=(k == PB))
                        last.then_inc(sem("pv_ready" + x), 1)
                    for g in range(2):
                        pe.wait_ge(sem("oN_ready" + x + str(g)), b + 1)
                        flip(PS[:, 5 + 2 * g, 0:P], oN[:, g, :]).then_inc(sem("oT_ready" + x), 1)

                turn_keys(0)
                with pe.Fori(0, DB - 1) as b:
                    stream(b, True)
                stream(DB - 1, False)

            pe.sem_inc(sem("o_readyA"), 1)
            pe.sem_inc(sem("o_readyB"), 1)
            pe.wait_ge(setup_in, 16 * 9)
            flip(PS[:, 7, 0:65], gN[0:65, :], 65).then_inc(sem("g_turned"), 1)
            for k in range(KB):
                for g, blocks in enumerate((range(0, 4), range(4, 5))):
                    n = 2 * k + g
                    if n >= 4:
                        pe.wait_ge(sem("x_evac"), n - 3)
                    for j, t in enumerate(blocks):
                        last = flip(PS[:, n % 4, j * P:(j + 1) * P], xN[:, t, k * P:(k + 1) * P])
                    last.then_inc(sem("x_turned"), 1)
            pe.wait_ge(sem("x_evac"), 2 * KB)
            pe.wait_ge(sem("ones_made"), 3)
            stats(0)
            ffn(0, BASE["ffn0"], 0)
            stats(1)
            pe.wait_ge(sem("xn_ready"), primed(2 * KB))
            with pe.Fori(0, 6) as n:
                token_tile(BASE["qkv"], 0, n)
            pe.wait_ge(sem("rope_done"), 2)
            pe.wait_ge(sem("rows_read"), 7 * TB)
            head_transposes("A", nat, 2, None)
            pe.wait_ge(sem("ht_actA"), 16)
            pe.wait_ge(sem("ht_dveA"), 16)
            prompt("A")
            pe.wait_ge(sem("o_readA"), primed(PAIR))
            pe.wait_ge(sem("own_in"), 16)
            sample("A")
            with pe.Fori(0, PAIR // 2) as i:
                for u in range(2):
                    pe.wait_ge(sem("o_squared"), i * 2 + u + 1)
                    pe.wait_ge(sem("oA_split"), primed(i * 2))
                    for h in range(2):
                        last = pe.matmul(pair(u)[:, h, :], ones_e[:, :], (t0, t1)[u][:, h * HT:(h + 1) * HT], start=True, stop=True)
                    last.then_inc(sem("o_mean"), 1)
            pe.wait_ge(sem("oA_split"), primed(PAIR))
            down(BASE["oa"], KB, xn_hi, xn_lo)
            stats(2)
            ffn(1, BASE["ffn1"], 2)
            stats(3)
            pe.wait_ge(sem("xn_ready"), primed(4 * KB))
            with pe.Fori(0, 4) as n:
                token_tile(BASE["kv"], 6, n)
            pe.wait_ge(w_split, BASE["wf"] + 1)
            stationary_tile(BASE["wf"] % 2, KB, xn_hi, xn_lo, pair(3))
            pe.wait_ge(sem("rows_read"), 11 * TB)
            head_transposes("B", nat, 1, None)
            pe.wait_ge(sem("logf_in"), 64)
            pe.wait_ge(sem("ht_actB"), 8)
            pe.wait_ge(sem("ht_dveB"), 8)
            for k in range(PB):
                last = flip(PS[:, 1, k * P:(k + 1) * P], LN[:, k, :])
            last.then_inc(sem("LT_ready"), 1)
            pe.wait_ge(sem("logf_done"), 1)
            for t in range(TB):
                last = flip(PS[:, 2, t * HB:(t + 1) * HB], lfT[:, t * P:(t + 1) * P], HB)
            last.then_inc(sem("lfN_ready"), 1)
            pe.wait_ge(sem("EX_done"), 1)
            pe.matmul(PS[:, 3, 0:DS], EX, cst[:, STEP:STEP + DS], start=True, stop=True).then_inc(sem("new_ready"), 1)
            pe.wait_ge(sem("new_read"), 1)
            ffn(2, BASE["ffn2"], 4)
            stats(4)
            pe.wait_ge(sem("xn_ready"), primed(6 * KB))
            down(BASE["qb"], KB, xn_hi, xn_lo)
            pe.wait_ge(sem("qT_copied"), 1)
            prompt("B")
            pe.wait_ge(sem("o_readB"), primed(PAIR))
            sample("B")
            pe.wait_ge(sem("oB_split"), PAIR)
            down(BASE["ob"], KB, xn_hi, xn_lo)
            stats(5)
            ffn(3, BASE["ffn3"], 6)
            stats(6)
            for k in range(KB):
                pe.wait_ge(sem("y_ready"), k + 1)
                for g, blocks in enumerate((range(0, 4), range(4, 5))):
                    n = 2 * k + g
                    if n >= 4:
                        pe.wait_ge(sem("y_evac"), n - 3)
                    for j, t in enumerate(blocks):
                        last = flip(PS[:, 4 + n % 4, j * P:(j + 1) * P], yT[:, k, t * P:(t + 1) * P])
                    last.then_inc(sem("y_turned"), 1)

        @block.scalar
        def _(act):
            step = sem("act_step")
            count = Count()

            def norm(stat, n):
                if stat is not None:
                    act.wait_ge(sem("mean_ready"), stat + 1)
                    act.activation(halves(t0[:, :]), pair(0), ACT.Sqrt, bias=eps).then_inc(sem("root_ready"), 1)
                if n == 7:
                    return
                with act.Fori(0, KB // 2) as i:
                    for u in range(2):
                        act.wait_ge(sem("scaled"), n * KB + i * 2 + u + 1)
                        act.activation(xn_hi[:, i * 2 + u, :], (t0, t2)[u][:, :], ACT.Copy).then_inc(sem("hi_ready"), 1)

            def ffn(f, base):
                for g in range(GRP):
                    at, blk = base + g * (2 * FB + KB), (f * GRP + g) * FB
                    with act.Fori(0, FB) as i:
                        act.wait_ge(w_used, at + i * 2 + 1)
                        act.wait_ge(sem("up_read"), primed(blk + i))
                        act.activation(halves(t0[:, :]), pair(0), ACT.Silu).then_inc(sem("gate_read"), 1)

            def heads(x, parts):
                for w in range(parts):
                    dst = (qT, kT)[w] if parts == 2 else kT
                    for h in range(PAIR):
                        act.wait_ge(sem("ht_ready" + x), (w * PAIR + h) * 2 + 2)
                        act.activation(dst[:, h, NP:T], PS[:, (2 * h + 1) % 4, 0:P], ACT.Copy).then_inc(sem("ht_act" + x), 1)

            def prompt(x):
                p_ready = sem("p_ready" + x)
                with act.Fori(0, PAIR) as h:
                    act.wait_ge(sem("o_ready" + x), primed(h))
                    act.activation(qh, qT[:, h, 0:NP], ACT.Copy)
                    act.activation(kh, kT[:, h, 0:NP], ACT.Copy)
                    act.activation(vh, vN[:, 0:PB, bass.ds(h * P, P)], ACT.Copy).then_inc(sem("staged" + x), 1)

                    def exps(t):
                        n = (t + 1) * P
                        act.wait_ge(sem("nb_ready" + x), h * 4 + t + 1)
                        for c in range(2):
                            src = PS[:, 2 * (t % 2) + c, 0:n] if x == "A" else PR[:, t % 2, c, 0:n]
                            last = act.activation(PR[:, t % 2, c, 0:n], src, ACT.Exp, bias=st[:, t % 2, 2 + c:3 + c],
                                                  scale=SCALE if x == "A" else 1.0, accum_out=st[:, t % 2, 4 + c:5 + c])
                        last.then_inc(sem("exp_done" + x), 1)

                    def turned(t):
                        act.wait_ge(sem("pt_ready" + x), h * 4 + t + 1)
                        for c in range(1 if x == "A" else 2):
                            last = act.activation(pT[:, c, 0:t + 1, t * P:(t + 1) * P],
                                                  PS[:, 4 + c, 0:(t + 1) * P].rearrange("p (k q) -> p k q", q=P), ACT.Copy)
                        last.then_inc(sem("pt_read" + x), 1)

                    exps(0)
                    exps(1)
                    turned(0)
                    exps(2)
                    turned(1)
                    exps(3)
                    turned(2)
                    turned(3)

            def sample(x):
                def stage(b):
                    at = bass.ds(b * DS + NP, DS)
                    act.activation(qbd[0:64, :, 0:DS], qT[0:64, :, at], ACT.Copy)
                    act.activation(qbd[64:P, :, DS:2 * DS], qT[64:P, :, at], ACT.Copy).then_inc(sem("q_staged" + x), 1)

                def keys(b):
                    for h in range(0, PAIR, 2):
                        act.wait_ge(sem("kt_ready" + x), b * 8 + h + 1)
                        act.activation(kTc[:, h, :], PS[:, h % 4, :], ACT.Copy).then_inc(sem("kt_act" + x), 1)

                def stream(b, following):
                    for g in range(2):
                        act.wait_ge(sem("snb_ready" + x), b * 2 + g + 1)
                        p = (t0, t1)[g][:, :]
                        act.activation(p, wide(4 + 2 * g) if x == "A" else p, ACT.Exp, bias=st[:, g, 2:3],
                                       scale=SCALE if x == "A" else 1.0, accum_out=st[:, g, 4:5]).then_inc(sem("sexp_done" + x), 1)
                    if following:
                        stage(b + 1)
                        keys(b + 1)
                    act.wait_ge(sem("pd_ready" + x), b * 2 + 1)
                    act.activation(t2[:, :], wide(0), ACT.Copy).then_inc(sem("pd_read" + x + "0"), 1)
                    act.wait_ge(sem("pv_ready" + x), b * 2 + 1)
                    for j in range(4):
                        rows = slice(32 * j, 32 * j + 32)
                        last = act.activation(oN[rows, 0, :], PS[rows, 4, j * P:(j + 1) * P], ACT.Copy)
                    last.then_inc(sem("oN_ready" + x + "0"), 1)

                act.wait_ge(sem("qbd_clear" + x), 1)
                stage(0)
                keys(0)
                with act.Fori(0, DB - 1) as b:
                    stream(b, True)
                stream(DB - 1, False)

            act.wait_ge(sem("lam_sums"), 1)
            act.activation(small[:, 4:6], small[:, 6:8], ACT.Exp).then_inc(sem("lam_exps"), 1)
            eps = small[:, 10:11]
            norm(0, 0)
            ffn(0, BASE["ffn0"])
            norm(1, 1)
            act.wait_ge(sem("rope_done"), 2)
            rows = "l b (t p) h c d -> p (l b t) (h c d)"
            act.dma_start(ak_prompt.rearrange(rows, p=P), nat[:, 1, 0:4, :]).then_inc(sem("ak_stored"), 16)
            act.dma_start(ak_sample.rearrange("l b t h c d -> (l b t) (h c d)"), nat[:, 1, 4, :]).then_inc(sem("ak_stored"), 16)
            act.wait_ge(sem("rows_read"), 7 * TB)
            act.dma_start(av_prompt.rearrange("l b (t p) h e -> p (l b t) (h e)", p=P), vN[:, 0:4, :]).then_inc(sem("av_stored"), 16)
            act.dma_start(av_sample.rearrange("l b t h e -> (l b t) (h e)"), vN[:, 4, :]).then_inc(sem("av_stored"), 16)
            heads("A", 2)
            act.wait_ge(sem("ak_stored"), 32)
            prompt("A")
            sample("A")
            with act.Fori(0, PAIR // 2) as i:
                for u in range(2):
                    act.wait_ge(sem("oT_readA"), primed(2 * DB))
                    act.wait_ge(sem("oA_split"), primed(i * 2))
                    act.activation((t0, t1)[u][:, :], oT[:, i * 2 + u, :], ACT.Square).then_inc(sem("o_squared"), 1)
                for u in range(2):
                    act.wait_ge(sem("o_mean"), i * 2 + u + 1)
                    act.activation(halves((t0, t1)[u][:, :]), pair(u), ACT.Sqrt, bias=eps).then_inc(sem("o_root"), 1)
            norm(2, 2)
            ffn(1, BASE["ffn1"])
            norm(3, 3)
            act.wait_ge(sem("rows_read"), 9 * TB)
            act.dma_start(bk_prompt.rearrange("b (t p) h d -> p (b t) (h d)", p=P), nat[:, 0, 0:4, :]).then_inc(sem("bk_stored"), 16)
            act.dma_start(bk_sample.rearrange("b t h d -> (b t) (h d)"), nat[:, 0, 4, :]).then_inc(sem("bk_stored"), 16)
            act.wait_ge(sem("rows_read"), 11 * TB)
            act.dma_start(bv_prompt.rearrange("b (t p) h d -> p (b t) (h d)", p=P), vN[:, 0:4, :]).then_inc(sem("bv_stored"), 16)
            act.dma_start(bv_sample.rearrange("b t h d -> (b t) (h d)"), vN[:, 4, :]).then_inc(sem("bv_stored"), 16)
            act.wait_ge(sem("absz_ready"), 1)
            act.activation(lf2, lf1, ACT.Exp, scale=-1.0).then_inc(step, 1)
            act.wait_ge(step, count.next())
            act.activation(lf1, lf2, ACT.Ln, bias=1.0).then_inc(sem("ln_ready"), 1)
            heads("B", 1)
            act.wait_ge(sem("lfN_read"), 1)
            act.dma_start(bf_prompt.rearrange("b (t p) h -> p (b t) h", p=P), lfN[:, 0:4, :]).then_inc(sem("bf_stored"), 16)
            act.dma_start(bf_sample.rearrange("b t h -> (b t) h"), lfN[:, 4, :]).then_inc(sem("bf_stored"), 16)
            act.dma_start(f_prompt_scr, FCp).then_inc(sem("bf_stored"), 16)
            act.wait_ge(sem("LO_ready"), 1)
            act.dma_start(f_sample_scr, LO).then_inc(sem("bf_stored"), 16)
            norm(None, 4)
            ffn(2, BASE["ffn2"])
            norm(4, 5)
            act.wait_ge(sem("qT_copied"), 1)
            prompt("B")
            sample("B")
            with act.Fori(0, PAIR) as h:
                act.wait_ge(sem("oT_readB"), primed(2 * DB))
                act.activation(xn_hi[:, h, :], oT[:, h, :], ACT.Copy).then_inc(sem("oB_hi"), 1)
            norm(5, 6)
            ffn(3, BASE["ffn3"])
            norm(6, 7)
            for t in range(TB):
                act.wait_ge(sem("y_evac"), 2 * KB)
            act.dma_start(y_prompt[0].rearrange("(t p) d -> p t d", p=P), yN[:, 0:4, :]).then_inc(sem("y_stored"), 16)
            act.dma_start(y_sample.rearrange("b t d -> (b t) d"), yN[:, 4, :]).then_inc(sem("y_stored"), 16)
            for name, n in (("ak_stored", 2), ("av_stored", 2), ("bk_stored", 2), ("bv_stored", 2), ("bf_stored", 4), ("y_stored", 2)):
                act.wait_ge(sem(name), 16 * n)

        @block.vector
        def _(dve):
            step = sem("dve_step")
            count = Count()

            def reciprocal_root():
                dve.reciprocal(t1[:, :], t0[:, :]).then_inc(step, 1)
                dve.wait_ge(step, count.next())

            def norm(stat, n, g):
                if stat is not None:
                    dve.wait_ge(sem("root_ready"), stat + 1)
                    reciprocal_root()
                with dve.Fori(0, KB // 2) as i:
                    dve.wait_ge(sem("xn_ready"), primed(i * 2 + n * KB))
                    for u in range(2):
                        k = i * 2 + u
                        dve.scalar_tensor_tensor(out=(t0, t2)[u][:, :], in0=xT[:, k, :], scalar=gT[:, bass.ds(k + 8 * g, 1)],
                                                 in1=t1[:, :], op0=ALU.mult, op1=ALU.mult).then_inc(sem("scaled"), 1)
                    for u in range(2):
                        k = i * 2 + u
                        dve.wait_ge(sem("hi_ready"), n * KB + k + 1)
                        dve.tensor_tensor(xn_lo[:, k, :], (t0, t2)[u][:, :], xn_hi[:, k, :].bitcast(F32),
                                          ALU.subtract).then_inc(sem("xn_ready"), 1)
                dve.wait_ge(sem("xn_ready"), primed((n + 1) * KB))

            def add_square(x):
                dve.tensor_tensor(t2[:, :], x, x, ALU.mult).then_inc(step, 1)
                dve.wait_ge(step, count.next())
                dve.tensor_tensor(sqacc[:, :], sqacc[:, :], t2[:, :], ALU.add).then_inc(step, 1)
                dve.wait_ge(step, count.next())

            def clear_squares():
                dve.memset(sqacc[:, :], 0.0).then_inc(step, 1)
                dve.wait_ge(step, count.next())

            def add_down(at, factor, squares):
                if squares:
                    clear_squares()
                with dve.Fori(0, KB // 2) as m, count.loop(m, KB // 2, 4 if squares else 0):
                    for u in range(2):
                        dve.wait_ge(w_used, at + m * 2 + u + 1)
                        x = xT[:, m * 2 + u, :]
                        dve.scalar_tensor_tensor(out=halves(x), in0=pair(2 + u), scalar=factor, in1=halves(x),
                                                 op0=ALU.mult, op1=ALU.add).then_inc(sem("down_read"), 1)
                        dve.wait_ge(sem("down_read"), sums[0] + m * 2 + u + 3)
                        if squares:
                            add_square(x)
                sums[0] += KB
                if squares:
                    dve.sem_inc(sem("squares_summed"), 1)

            sums = [0]

            def ffn(f, base):
                for g in range(GRP):
                    at, blk = base + g * (2 * FB + KB), (f * GRP + g) * FB
                    with dve.Fori(0, FB) as i, count.loop(i, FB, 1):
                        dve.wait_ge(w_used, at + i * 2 + 2)
                        dve.wait_ge(sem("gate_read"), blk + i + 1)
                        dve.wait_ge(sem("act_ready"), primed(blk + i))
                        dve.tensor_tensor(halves(t1[:, :]), halves(t0[:, :]), pair(1), ALU.mult).then_inc(sem("up_read"), 1)
                        dve.wait_ge(sem("up_read"), primed(blk + i + 1))
                        dve.tensor_copy(act_hi[:, i, :], t1[:, :]).then_inc(step, 1)
                        dve.wait_ge(step, count.next())
                        dve.tensor_tensor(act_lo[:, i, :], t1[:, :], act_hi[:, i, :].bitcast(F32),
                                          ALU.subtract).then_inc(sem("act_ready"), 1)
                    add_down(at + 2 * FB, 0.5, g == GRP - 1)

            def rows_out(dst, at, n0, tiles):
                with dve.Fori(0, tiles) as n:
                    dve.wait_ge(w_used, n * 4 + (at + 4 * n0 + 4))
                    for t in range(TB):
                        dve.tensor_copy(dst[:, t, bass.ds(n * 512, 512)], PS[:, t, :]).then_inc(sem("rows_read"), 1)

            def rope(x):
                v = x.rearrange("p t (m d) -> p t m d", d=64)
                x1, x2 = v[:, :, :, 0:8], v[:, :, :, 8:16]
                shape = [P, TB, 16, 8]
                cos = rope_consts[:, :, 0:8].rearrange("p t (o d) -> p t o d", o=1).to_broadcast(shape)
                sin = rope_consts[:, :, 8:16].rearrange("p t (o d) -> p t o d", o=1).to_broadcast(shape)
                tmp = [t[:, :].rearrange("p (t m d) -> p t m d", t=TB, d=8) for t in (t0, t1, t2, sqacc)]
                for out, a, b in zip(tmp, (x1, x2, x2, x1), (cos, sin, cos, sin)):
                    dve.tensor_tensor(out, a, b, ALU.mult).then_inc(step, 1)
                    seen = count.next()
                dve.wait_ge(step, seen)
                dve.tensor_tensor(x1, tmp[0], tmp[1], ALU.subtract)
                dve.tensor_tensor(x2, tmp[2], tmp[3], ALU.add).then_inc(sem("rope_done"), 1)

            def heads(x, parts):
                for w in range(parts):
                    dst = (qT, kT)[w] if parts == 2 else kT
                    for h in range(PAIR):
                        dve.wait_ge(sem("ht_ready" + x), (w * PAIR + h) * 2 + 1)
                        dve.tensor_copy(dst[:, h, 0:NP], PS[:, (2 * h) % 4, :]).then_inc(sem("ht_dve" + x), 1)

            def prompt(x):
                with dve.Fori(0, PAIR) as h, count.loop(h, PAIR, 4 * (4 if x == "A" else 3)):
                    def peak(t):
                        n, s = (t + 1) * P, st[:, t % 2, :]
                        dve.wait_ge(sem("s_ready" + x), h * 4 + t + 1)
                        for c in range(2):
                            src = PS[:, 2 * (t % 2) + c, 0:n]
                            if x == "A":
                                last = dve.reduce_max(s[:, c:c + 1], src, AX)
                            else:
                                if c == 0:
                                    dve.sem_inc(sem("dve_passed"), 1)
                                last = dve.tensor_tensor_reduce(out=PR[:, t % 2, c, 0:n], in0=src, in1=FP[:, c, 0:n],
                                                                scale=SCALE, scalar=-3e38, op0=ALU.add, op1=ALU.max,
                                                                accum_out=s[:, c:c + 1])
                        last.then_inc(step, 1)
                        dve.wait_ge(step, count.next())
                        dve.tensor_scalar(s[:, 2:4], s[:, 0:2], -SCALE if x == "A" else -1.0, None, ALU.mult).then_inc(
                            sem("nb_ready" + x), 1)

                    def combine(t):
                        n, s = (t + 1) * P, st[:, t % 2, :]
                        p0, p1 = PR[:, t % 2, 0, 0:n], PR[:, t % 2, 1, 0:n]
                        dve.wait_ge(sem("exp_done" + x), h * 4 + t + 1)
                        dve.reciprocal(s[:, 4:6], s[:, 4:6]).then_inc(step, 1)
                        dve.wait_ge(step, count.next())
                        if x == "A":
                            dve.tensor_tensor(s[:, 5:6], s[:, 5:6], neg_lam, ALU.mult).then_inc(step, 1)
                            dve.tensor_scalar(p0, p0, s[:, 4:5], None, ALU.mult).then_inc(step, 1)
                            count.next()
                            dve.wait_ge(step, count.next())
                            dve.scalar_tensor_tensor(out=p0, in0=p1, scalar=s[:, 5:6], in1=p0, op0=ALU.mult,
                                                     op1=ALU.add).then_inc(sem("p_readyA"), 1)
                        else:
                            dve.tensor_scalar(p0, p0, s[:, 4:5], None, ALU.mult).then_inc(step, 1)
                            count.next()
                            dve.tensor_scalar(p1, p1, s[:, 5:6], None, ALU.mult).then_inc(sem("p_readyB"), 1)

                    if x == "B":
                        dve.wait_ge(sem("row_in"), h * 32 + 32)
                    peak(0)
                    peak(1)
                    combine(0)
                    peak(2)
                    combine(1)
                    peak(3)
                    if x == "B":
                        dve.sem_inc(sem("rows_free"), 1)
                    combine(2)
                    combine(3)
                    dve.wait_ge(sem("o_ready" + x), primed(h + 1))
                    dve.tensor_copy(oT[:, h, 0:NP], PS[:, 6, :]).then_inc(sem("o_read" + x), 1)

            def sample(x):
                def keys(b):
                    for h in range(1, PAIR, 2):
                        dve.wait_ge(sem("kt_ready" + x), b * 8 + h + 1)
                        dve.tensor_copy(kTc[:, h, :], PS[:, h % 4, :]).then_inc(sem("kt_dve" + x), 1)

                def stream(b, following):
                    for g in range(2):
                        s = st[:, g, :]
                        dve.wait_ge(sem("ss_ready" + x), b * 2 + g + 1)
                        if x == "A":
                            dve.reduce_max(s[:, 0:1], wide(4 + 2 * g), AX).then_inc(step, 1)
                            dve.wait_ge(step, count.next())
                        else:
                            dve.wait_ge(sem("f_inB"), b * 32 + 32)
                            dve.sem_inc(sem("dve_passed"), 1)
                            dve.tensor_tensor_reduce(out=(t0, t1)[g][:, :], in0=wide(4 + 2 * g), in1=FS[:, g, :], scale=SCALE,
                                                     scalar=-3e38, op0=ALU.add, op1=ALU.max,
                                                     accum_out=s[:, 0:1]).then_inc(sem("biasedB"), 1)
                            dve.wait_ge(sem("biasedB"), b * 2 + g + 1)
                        dve.tensor_scalar(s[:, 2:3], s[:, 0:1], -SCALE if x == "A" else -1.0, None, ALU.mult).then_inc(
                            sem("snb_ready" + x), 1)
                    for g in range(2):
                        s = st[:, g, :]
                        dve.wait_ge(sem("sexp_done" + x), b * 2 + g + 1)
                        dve.reciprocal(s[:, 5:6], s[:, 4:5]).then_inc(step, 1)
                        dve.wait_ge(step, count.next())
                        if x == "A":
                            dve.tensor_scalar(Cm[:, g, :], cst[:, SPREAD:SPREAD + P], s[:, 5:6], comp, ALU.mult,
                                              ALU.mult).then_inc(sem("norm_readyA"), 1)
                        else:
                            dve.tensor_scalar(Cm[:, g, :], ident, s[:, 5:6], None, ALU.mult).then_inc(sem("norm_readyB"), 1)
                    if following:
                        keys(b + 1)
                    dve.wait_ge(sem("pd_ready" + x), b * 2 + 2)
                    dve.tensor_copy(sqacc[:, :], wide(2)).then_inc(sem("pd_read" + x + "1"), 1)
                    dve.wait_ge(sem("pv_ready" + x), b * 2 + 2)
                    for j in range(4):
                        rows = slice(32 * j, 32 * j + 32)
                        last = dve.tensor_copy(oN[rows, 1, :], PS[rows, 6, j * P:(j + 1) * P])
                    last.then_inc(sem("oN_ready" + x + "1"), 1)
                    for g in range(2):
                        dve.wait_ge(sem("oT_ready" + x), b * 2 + g + 1)
                        src = PS[:, 5 + 2 * g, 0:P].rearrange("p (j c q) -> p j c q", j=4, c=2)
                        at = bass.ds(b * DS + NP, DS)
                        if x == "A":
                            last = dve.tensor_copy(oT[:, 4 * g:4 * g + 4, at], src[:, :, 0, :])
                        else:
                            for c in range(2):
                                e = slice(64 * c, 64 * c + 64)
                                last = dve.tensor_copy(oT[e, 4 * g:4 * g + 4, at], src[e, :, c, :])
                        last.then_inc(sem("oT_read" + x), 1)

                dve.memset(qbd, 0.0).then_inc(sem("qbd_clear" + x), 1)
                keys(0)
                with dve.Fori(0, DB - 1) as b, count.loop(b, DB - 1, 4 if x == "A" else 2):
                    stream(b, True)
                stream(DB - 1, False)

            dve.memset(ones_d[:, :], 1.0 / D).then_inc(sem("ones_made"), 1)
            dve.memset(ones_e[:, :], 1.0 / P).then_inc(sem("ones_made"), 1)
            dve.memset(small[:, 10:11], EPS).then_inc(sem("ones_made"), 1)
            for name in ("o_readA", "o_readB", "oT_readA", "oT_readB", "oA_split", "up_read", "xn_ready", "act_ready"):
                dve.sem_inc(sem(name), 1)
            dve.sem_inc(sem("down_read"), 2)
            dve.sem_inc(sem("rows_read"), TB)
            dve.wait_ge(setup_in, 16 * 9)
            for c in range(2):
                dve.tensor_tensor_reduce(out=t0[:, 64 * c:64 * c + 64], in0=lamN[:, 128 * c:128 * c + 64],
                                         in1=lamN[:, 128 * c + 64:128 * c + 128], scale=1.0, scalar=0.0, op0=ALU.mult,
                                         op1=ALU.add, accum_out=small[:, 6 + c:7 + c]).then_inc(sem("lam_sums" if c else "lam_sum0"), 1)
            clear_squares()
            for k in range(KB):
                for g in range(2):
                    n = 2 * k + g
                    dve.wait_ge(sem("x_turned"), n + 1)
                    cols = slice(0, NP) if g == 0 else slice(NP, T)
                    dve.tensor_copy(xT[:, k, cols], PS[:, n % 4, 0:NP if g == 0 else P]).then_inc(sem("x_evac"), 1)
                dve.wait_ge(sem("x_evac"), 2 * k + 2)
                add_square(xT[:, k, :])
            dve.sem_inc(sem("squares_summed"), 1)
            dve.wait_ge(sem("g_turned"), 1)
            dve.tensor_copy(gT[:, 0:65], PS[:, 7, 0:65]).then_inc(step, 1)
            dve.wait_ge(step, count.next())
            dve.tensor_scalar(gsub, GSUB, 1.0 - LAM_INIT, None, ALU.mult).then_inc(step, 1)
            count.next()
            dve.wait_ge(sem("lam_exps"), 1)
            dve.tensor_tensor(small[:, 8:9], small[:, 5:6], small[:, 4:5], ALU.subtract).then_inc(step, 1)
            dve.wait_ge(step, count.next())
            dve.tensor_scalar(neg_lam, small[:, 8:9], -LAM_INIT, None, ALU.add).then_inc(step, 1)
            dve.wait_ge(step, count.next())
            dve.scalar_tensor_tensor(out=comp, in0=cst[:, COMP1:COMP1 + 1], scalar=neg_lam, in1=cst[:, COMP0:COMP0 + 1],
                                     op0=ALU.mult, op1=ALU.add).then_inc(step, 1)
            dve.wait_ge(step, count.next())
            norm(0, 0, 0)
            ffn(0, BASE["ffn0"])
            norm(1, 1, 1)
            rows_out(nat[:, 0], BASE["qkv"], 0, 2)
            dve.wait_ge(sem("rows_read"), 3 * TB)
            rope(nat[:, 0])
            rows_out(nat[:, 1], BASE["qkv"], 2, 2)
            dve.wait_ge(sem("rows_read"), 5 * TB)
            dve.wait_ge(sem("rope_done"), 1)
            rope(nat[:, 1])
            rows_out(vN, BASE["qkv"], 4, 2)
            heads("A", 2)
            prompt("A")
            sample("A")
            with dve.Fori(0, PAIR // 2) as i, count.loop(i, PAIR // 2, 6):
                for u in range(2):
                    h, t = i * 2 + u, (t0, t1)[u][:, :]
                    dve.wait_ge(sem("o_root"), h + 1)
                    dve.reciprocal(t, t).then_inc(step, 1)
                    dve.wait_ge(step, count.next())
                    dve.wait_ge(sem("oA_split"), primed(h))
                    dve.scalar_tensor_tensor(out=t2[:, :], in0=oT[:, h, :], scalar=gsub, in1=t, op0=ALU.mult,
                                             op1=ALU.mult).then_inc(step, 1)
                    dve.wait_ge(step, count.next())
                    dve.tensor_copy(xn_hi[:, h, :], t2[:, :]).then_inc(step, 1)
                    dve.wait_ge(step, count.next())
                    dve.tensor_tensor(xn_lo[:, h, :], t2[:, :], xn_hi[:, h, :].bitcast(F32), ALU.subtract).then_inc(
                        sem("oA_split"), 1)
            add_down(BASE["oa"], 1.0, True)
            norm(2, 2, 2)
            ffn(1, BASE["ffn1"])
            norm(3, 3, G_KV)
            rows_out(nat[:, 0], BASE["kv"], 0, 2)
            dve.wait_ge(sem("av_stored"), 32)
            rows_out(vN, BASE["kv"], 2, 2)
            dve.wait_ge(w_used, BASE["wf"] + 1)
            zt = lfT
            dve.tensor_scalar(halves(zt), pair(3)[0:HB], small[0:HB, 3:4], None, ALU.add).then_inc(step, 1)
            dve.wait_ge(step, count.next())
            dve.scalar_tensor_tensor(out=lf1, in0=zt, scalar=-1.0, in1=zt, op0=ALU.mult, op1=ALU.max).then_inc(
                sem("absz_ready"), 1)
            heads("B", 1)
            dve.wait_ge(sem("LT_ready"), 1)
            dve.tensor_copy(LT, PS[:, 1, :]).then_inc(step, 1)
            count.next()
            dve.wait_ge(sem("ln_ready"), 1)
            dve.scalar_tensor_tensor(out=lfT, in0=zt, scalar=0.0, in1=lf1, op0=ALU.min, op1=ALU.subtract).then_inc(
                sem("logf_done"), 1)
            dve.wait_ge(sem("logf_done"), 1)
            ones16 = lf2[:, 0:NP]
            dve.memset(ones16, 1.0).then_inc(step, 1)
            dve.wait_ge(step, count.next())
            dve.tensor_tensor_scan(FCp, ones16, lfT[:, 0:NP], 0.0, ALU.mult, ALU.add).then_inc(step, 1)
            dve.memset(sqacc[:, 0:NP], 1.0).then_inc(step, 1)
            count.next()
            dve.wait_ge(step, count.next())
            dve.tensor_scalar(FCp, FCp, -1.0 / SCALE, None, ALU.mult).then_inc(step, 1)
            dve.tensor_tensor_scan(FC[:, 0:PAST], sqacc[:, 0:PAST], LT, 0.0, ALU.mult, ALU.add).then_inc(step, 1)
            count.next()
            count.next()
            dve.wait_ge(sem("lfN_ready"), 1)
            dve.tensor_copy(lfN, PS[:, 2, 0:TB * HB].rearrange("p (t h) -> p t h", t=TB)).then_inc(sem("lfN_read"), 1)
            dve.wait_ge(sem("lfN_read"), 1)
            same = cst[:, SAME:SAME + P].rearrange("p (b h) -> p b h", b=DB)
            new = lfN[:, TB - 1:TB, :].to_broadcast([P, DB, HB])
            dve.tensor_tensor(EX.rearrange("p (b h) -> p b h", b=DB), same, new, ALU.mult).then_inc(sem("EX_done"), 1)
            dve.wait_ge(sem("new_ready"), 1)
            dve.tensor_copy(small[:, 16:32], PS[:, 3, 0:DS]).then_inc(sem("new_read"), 1)
            dve.wait_ge(sem("new_read"), 1)
            dve.wait_ge(step, count.off + count.n)
            dve.tensor_tensor_scan(FC[:, PAST:PAST + DS], sqacc[:, 0:DS], small[:, 16:32], FC[:, PAST - 1:PAST], ALU.mult,
                                   ALU.add).then_inc(step, 1)
            dve.wait_ge(step, count.next())
            dve.tensor_scalar(LO[:, 0:PAST], FC[:, 0:PAST], -1.0 / SCALE, None, ALU.mult)
            mine = FC[:, PAST:PAST + DS].rearrange("p (o t) -> p o t", o=1).to_broadcast([P, DB, DS])
            dve.tensor_tensor(EX.rearrange("p (b h) -> p b h", b=DB), same, mine, ALU.mult).then_inc(step, 1)
            dve.wait_ge(step, count.next())
            dve.scalar_tensor_tensor(out=LO[:, PAST:T], in0=EX, scalar=-1.0 / SCALE, in1=cst[:, OTHER:OTHER + P],
                                     op0=ALU.mult, op1=ALU.add).then_inc(sem("LO_ready"), 1)
            norm(None, 4, 3)
            dve.wait_ge(sem("bk_stored"), 32)
            dve.wait_ge(sem("bf_stored"), 64)
            ffn(2, BASE["ffn2"])
            norm(4, 5, 4)
            with dve.Fori(0, KB // 2) as m:
                for u in range(2):
                    dve.wait_ge(w_used, BASE["qb"] + 1 + m * 2 + u)
                    dve.tensor_copy(halves(qraw[:, m * 2 + u, :]), pair(2 + u)).then_inc(sem("down_read"), 1)
            sums[0] += KB
            dve.wait_ge(sem("down_read"), sums[0] + 2)
            dve.sem_inc(sem("rows_free"), 1)
            dve.tensor_copy(qT[:, :, :], qraw).then_inc(sem("qT_copied"), 1)
            prompt("B")
            sample("B")
            with dve.Fori(0, PAIR) as h:
                dve.wait_ge(sem("oB_hi"), h + 1)
                dve.tensor_tensor(xn_lo[:, h, :], oT[:, h, :], xn_hi[:, h, :].bitcast(F32), ALU.subtract).then_inc(
                    sem("oB_split"), 1)
            add_down(BASE["ob"], 1.0, True)
            norm(5, 6, 5)
            ffn(3, BASE["ffn3"])
            dve.wait_ge(sem("root_ready"), 6 + 1)
            reciprocal_root()
            for k in range(KB):
                dve.scalar_tensor_tensor(out=yT[:, k, :], in0=xT[:, k, :], scalar=gcol(G_FINAL, k), in1=t1[:, :],
                                         op0=ALU.mult, op1=ALU.mult).then_inc(sem("y_ready"), 1)
            for k in range(KB):
                for g in range(2):
                    n = 2 * k + g
                    dve.wait_ge(sem("y_turned"), n + 1)
                    blocks = slice(0, 4) if g == 0 else slice(4, 5)
                    src = PS[:, 4 + n % 4, 0:NP if g == 0 else P].rearrange("p (t c) -> p t c", c=P)
                    dve.tensor_copy(yN[:, blocks, k * P:(k + 1) * P], src).then_inc(sem("y_evac"), 1)


_INS = ['x_prompt', 'x_sample', 'cache_a_k', 'cache_a_v', 'cache_b_k', 'cache_b_v', 'cache_b_logf', 'g_norm', 'w_ffn_gate',
        'w_ffn_up', 'w_ffn_down', 'w_qkv_a', 'lambda_a', 'g_sub_a', 'w_o_a', 'g_kv_b', 'w_kv_b', 'w_f_b', 'b_f_b', 'w_q_b',
        'w_o_b', 'g_final']
_OUTS = [(1, NP, D), (DB, DS, D), (1, 1, NP, 8, 2, 64), (1, 1, NP, 8, 128), (1, NP, HB, 64), (1, NP, HB, 64), (1, NP, HB),
         (1, DB, DS, 8, 2, 64), (1, DB, DS, 8, 128), (DB, DS, HB, 64), (DB, DS, HB, 64), (DB, DS, HB)]


def shape_constants():
    import numpy as np
    p, j = np.arange(P)[:, None], np.arange(P)[None, :]
    c = np.zeros((P, NCONST), np.float32)
    c[:, IDENT:IDENT + P] = p == j
    c[:, CAUSAL:CAUSAL + P] = np.where(j > p, NEG, 0)
    c[:, CHUNKED:CHUNKED + P] = np.where((p < 64) & (j >= 64), NEG, 0)
    c[:, SPREAD:SPREAD + P] = (p // 32 == j // 32) & (p % 16 == j % 32)
    c[:, SAME:SAME + P] = p // 16 == j // 16
    c[:, OTHER:OTHER + P] = np.where(p // 16 == j // 16, 0, NEG)
    c[:, STEP:STEP + P] = p % 16 == j
    c[:, QSEL:QSEL + P] = p == j % 16
    c[:, QTRI:QTRI + P] = np.where(j % 16 > p, NEG, 0)
    c[:, COMP0] = (p[:, 0] // 16) % 2 == 0
    c[:, COMP1] = (p[:, 0] // 16) % 2 == 1
    inv = np.power(np.float32(500000.0), -np.arange(8, dtype=np.float32) * np.float32(2.0) / np.float32(16)).astype(np.float32)
    for t in range(TB):
        pos = (np.arange(P) + t * P if t < TB - 1 else PAST + np.arange(P) % DS).astype(np.float32)
        ang = (pos[:, None] * inv[None, :]).astype(np.float32).astype(np.float64)
        c[:, ROPE + 16 * t:ROPE + 16 * t + 8] = np.cos(ang)
        c[:, ROPE + 16 * t + 8:ROPE + 16 * t + 16] = np.sin(ang)
    own = np.where(np.arange(P)[None, :] // DS == np.arange(DB)[:, None], 0, NEG).astype(np.float32)
    return c, own.reshape(1, DB * P)


def kernel(**inputs):
    import numpy as _np
    import concourse.bacc as _bacc
    from concourse import mybir as _mybir
    from concourse.bass_utils import run_bass_kernel_spmd as _run

    nc = _bacc.Bacc("TRN2", target_bir_lowering=False, num_devices=1)
    arrays, args = {}, []
    consts = dict(zip(("shape_consts", "new_mask"), shape_constants()))
    for name in [*_INS, *consts]:
        a = _np.ascontiguousarray(inputs[name] if name in inputs else consts[name])
        arrays[f"in_{name}_dram"] = a
        args.append(nc.dram_tensor(f"in_{name}_dram", a.shape, _mybir.dt.from_np(a.dtype), kind="ExternalInput").ap())
    for i, shape in enumerate(_OUTS):
        args.append(nc.dram_tensor(f"out_{i}_dram", shape, F32, kind="ExternalOutput").ap())
    args.append(nc.dram_tensor("f_prompt_scr", (HB, NP), F32, kind="Internal").ap())
    args.append(nc.dram_tensor("f_sample_scr", (P, T), F32, kind="Internal").ap())
    yoco_stream_step(nc, *args)
    r = _run(nc, [arrays], core_ids=[0])
    return tuple(r.results[0][f"out_{i}_dram"] for i in range(len(_OUTS)))
```

```python
from contextlib import ExitStack, contextmanager

import concourse.bass as bass
from concourse import mybir

F32 = mybir.dt.float32
F32R = mybir.dt.float32r
ALU = mybir.AluOpType
ACT = mybir.ActivationFunctionType
AX = mybir.AxisListType.X

P = 128
D = 1024
KB = D // P
NP, DB, DS = 512, 8, 16
T = NP + DB * DS
TB = T // P
HT = T // 2
FF = 2816
GRP = 2
FB = FF // P // GRP
PAST = 512
PB = PAST // P
PAIR = 8
HB = 16
EPS = 1e-6
SCALE = 0.125
NEG = -1e30
LAM_INIT = 0.2

IDENT, CAUSAL, CHUNKED, SPREAD, SAME, OTHER, STEP, QSEL, QTRI = (i * P for i in range(9))
COMP0 = 9 * P
COMP1 = COMP0 + 1
ROPE = COMP0 + 2
NCONST = ROPE + TB * 16

FFN_TILES = GRP * (2 * FB + KB)
QKV_TILES, KV_TILES, SQ_TILES = 24, 16, 8
BASE = {}
_n = 0
for _name, _k in (("ffn0", FFN_TILES), ("qkv", QKV_TILES), ("oa", SQ_TILES), ("ffn1", FFN_TILES), ("kv", KV_TILES),
                  ("wf", 1), ("ffn2", FFN_TILES), ("qb", SQ_TILES), ("ob", SQ_TILES), ("ffn3", FFN_TILES)):
    BASE[_name] = _n
    _n += _k


def primed(n):
    return n + 1


class Count:

    def __init__(self):
        self.n, self.off = 0, 0

    def next(self):
        self.n += 1
        return self.off + self.n

    @contextmanager
    def loop(self, i, trips, per):
        n, off = self.n, self.off
        self.off = off + i * per
        yield
        assert self.n - n == per, (self.n - n, per)
        self.n, self.off = n + trips * per, off


def yoco_stream_step(nc, x_prompt, x_sample, cache_a_k, cache_a_v, cache_b_k, cache_b_v, cache_b_logf,
                     g_norm, w_ffn_gate, w_ffn_up, w_ffn_down, w_qkv_a, lambda_a, g_sub_a, w_o_a,
                     g_kv_b, w_kv_b, w_f_b, b_f_b, w_q_b, w_o_b, g_final, shape_consts, new_mask,
                     y_prompt, y_sample, ak_prompt, av_prompt, bk_prompt, bv_prompt, bf_prompt,
                     ak_sample, av_sample, bk_sample, bv_sample, bf_sample, f_prompt_scr, f_sample_scr):
    with ExitStack() as ctx:
        ctx.enter_context(nc.allow_non_contiguous_dma("gate biases and log-forget rows"))

        def sb(name, shape, dt=F32):
            return ctx.enter_context(nc.sbuf_tensor(name, shape, dt))

        def lent(*specs):
            with ExitStack() as s:
                return [s.enter_context(nc.sbuf_tensor(*spec)) for spec in specs]

        sems = {}

        def sem(name):
            if name not in sems:
                sems[name] = ctx.enter_context(nc.semaphore(name))
            return sems[name]

        xT = sb("xT", [P, KB, T])
        xn_hi, xn_lo = lent(("xn_hi", [P, KB, T], F32R), ("xn_lo", [P, KB, T], F32R))
        qT = sb("qT", [P, PAIR, T])
        oT = sb("oT", [P, PAIR, T])
        act_hi, act_lo = lent(("act_hi", [P, FB, T], F32R), ("act_lo", [P, FB, T], F32R))
        R1 = sb("R1", [P, 2 * FB * T])
        kT = sb("kT", [P, PAIR, T])
        vN = sb("vN", [P, TB, D])
        ring = lent(*((f"{n}{i}", [P, FB * P], dt) for n, dt in (("raw", F32), ("w_hi", F32R), ("w_lo", F32R))
                      for i in range(2)))
        raw, w_hi, w_lo = ring[0:2], ring[2:4], ring[4:6]
        R2 = sb("R2", [P, 6 * FB * P])
        cst = sb("cst", [P, NCONST])
        gT = sb("gT", [P, 68])
        t0 = sb("t0", [P, T])
        t1 = sb("t1", [P, T])
        t2 = sb("t2", [P, T])
        sqacc = sb("sqacc", [P, T])
        ones_d = sb("ones_d", [P, P])
        ones_e = sb("ones_e", [P, P])
        Cm = sb("Cm", [P, 2, P])
        st = sb("st", [P, 3, 8])
        small = sb("small", [P, 32])
        PS = ctx.enter_context(nc.psum_tensor("PS", [P, 8, 512], F32))

        ident = cst[:, IDENT:IDENT + P]
        nat = R1[:, 0:2 * TB * D].rearrange("p (w t c) -> p w t c", w=2, t=TB)
        Knat = R1[:, 0:4096].rearrange("p (k c) -> p k c", k=PB)
        kTc = R1[:, 4096:8192].rearrange("p (h k) -> p h k", h=PAIR)
        Vc = R1[:, 8192:12288].rearrange("p (k c) -> p k c", k=PB)
        qbd = R1[:, 12288:12544].rearrange("p (h m) -> p h m", h=PAIR)
        oN = R1[:, 12544:12800].rearrange("p (g m) -> p g m", g=2)
        FS = R1[:, 12800:14080].rearrange("p (g m) -> p g m", g=2)
        PR = R2[:, 0:1024].rearrange("p (c k) -> p c k", c=2)
        pT = R2[:, 1024:5120].rearrange("p (c k q) -> p c k q", c=2, k=PB)
        FP = R2[:, 5120:6144].rearrange("p (c k) -> p c k", c=2)
        qh = R2[:, 6144:6656]
        kh = R2[:, 6656:7168]
        vh = R2[:, 7168:7680].rearrange("p (k e) -> p k e", k=PB)
        xN = R1[:, 0:TB * D].rearrange("p (t c) -> p t c", t=TB)
        yT = R1[:, 0:KB * T].rearrange("p (k t) -> p k t", k=KB)
        yN = R1[:, KB * T:2 * KB * T].rearrange("p (t c) -> p t c", t=TB)
        gN = R1[:, 13312:13440]
        lamN = R1[:, 13440:13696]
        own = R1[0:1, 12800:13824]
        qraw = R1[:, 0:PAIR * T].rearrange("p (h t) -> p h t", h=PAIR)
        LN = R1[:, 5120:5632].rearrange("p (k m) -> p k m", k=PB)
        LT = R1[:, 5632:6144]
        lfT = R1[0:HB, 6144:6784]
        lf1 = R1[0:HB, 6784:7424]
        lf2 = R1[0:HB, 7424:8064]
        FCp = R1[0:HB, 8064:8576]
        lfN = R1[:, 8576:8656].rearrange("p (t h) -> p t h", t=TB)
        EX = R1[:, 8704:8832]
        FC = R1[:, 8832:9360]
        LO = R1[:, 9408:10048]
        rope_consts = cst[:, ROPE:ROPE + TB * 16].rearrange("p (t c) -> p t c", t=TB)

        def pair(n):
            return PS[:, 2 * n:2 * n + 2, 0:HT]

        def halves(ap):
            return ap.rearrange("p (b n) -> p b n", b=2)

        def wide(bank, n=T):
            return PS[:, bank:bank + 2, :].rearrange("p b n -> p (b n)")[:, 0:n]

        def gcol(j, k=None):
            return gT[:, 8 * j:8 * j + 8] if k is None else gT[:, 8 * j + k:8 * j + k + 1]

        GSUB = gT[:, 64:65]
        neg_lam, comp = small[:, 0:1], small[:, 1:2]
        gsub = small[:, 2:3]
        G_KV, G_FINAL = 6, 7

        w_loaded = [sem("w_loaded0"), sem("w_loaded1")]
        w_hi_made, w_split, w_used = sem("w_hi_made"), sem("w_split"), sem("w_used")
        setup_in, stored = sem("setup_in"), sem("stored")
        stores = [0]

        block = ctx.enter_context(nc.Block())

        @block.sync
        def _(sp):
            sp.dma_start(xN[:, 0:4, :], x_prompt[0].rearrange("(t p) d -> p t d", p=P)).then_inc(setup_in, 16)
            sp.dma_start(xN[:, 4, :], x_sample.rearrange("b t d -> (b t) d")).then_inc(setup_in, 16)
            sp.dma_start(cst[:, :], shape_consts).then_inc(setup_in, 16)
            sp.dma_start(gN[0:48, :], g_norm.rearrange("l j (k p) -> (l j k) p", p=P)).then_inc(setup_in, 16)
            sp.dma_start(gN[48:56, :], g_kv_b.rearrange("(k p) -> k p", p=P)).then_inc(setup_in, 16)
            sp.dma_start(gN[56:64, :], g_final.rearrange("(k p) -> k p", p=P)).then_inc(setup_in, 16)
            sp.dma_start(gN[64:65, :], g_sub_a).then_inc(setup_in, 16)
            sp.dma_start(lamN[:, :], lambda_a.rearrange("l c d -> l (c d)").to_broadcast([P, 4 * 64])).then_inc(setup_in, 16)
            sp.dma_start(small[0:HB, 3:4], b_f_b.rearrange("(h o) -> h o", o=1)).then_inc(setup_in, 16)

            def tile(n, slot, view, src):
                if not isinstance(n, int) or n >= 2:
                    sp.wait_ge(w_split, n - 1)
                sp.dma_start(view, src).then_inc(w_loaded[slot], 16)

            def cols(w, slot, at, kb=KB):
                return (raw[slot][:, 0:kb * P].rearrange("p (k m) -> p k m", k=kb),
                        w[:, bass.ds(at, P)].rearrange("(k p) m -> p k m", p=P))

            def load_ffn(f, base):
                l, j = f // 2, f % 2
                gate, up, down = w_ffn_gate[l, j], w_ffn_up[l, j], w_ffn_down[l, j]
                for g in range(GRP):
                    at = base + g * (2 * FB + KB)
                    first = 0
                    if at == 0:
                        tile(0, 0, *cols(gate, 0, 0))
                        tile(1, 1, *cols(up, 1, 0))
                        first = 1
                    with sp.Fori(first, FB) as i:
                        s = at % 2
                        tile(at + i * 2, s, *cols(gate, s, (i + g * FB) * P))
                        tile(at + i * 2 + 1, 1 - s, *cols(up, 1 - s, (i + g * FB) * P))
                    at += 2 * FB
                    rows = down[g * FB * P:(g + 1) * FB * P, :]
                    with sp.Fori(0, KB // 2) as m:
                        s = at % 2
                        tile(at + m * 2, s, *cols(rows, s, m * 2 * P, FB))
                        tile(at + m * 2 + 1, 1 - s, *cols(rows, 1 - s, m * 2 * P + P, FB))

            def load_square(w, base):
                with sp.Fori(0, KB // 2) as m:
                    s = base % 2
                    tile(base + m * 2, s, *cols(w, s, m * 2 * P))
                    tile(base + m * 2 + 1, 1 - s, *cols(w, 1 - s, m * 2 * P + P))

            def load_rows(w, base, n_tiles):
                with sp.Fori(0, n_tiles) as n:
                    for u in range(4):
                        s = (base + u) % 2
                        tile(base + n * 4 + u, s, raw[s][:, 0:1024].rearrange("p (k m) -> p k m", k=2),
                             w[u * 256:(u + 1) * 256, bass.ds(n * 512, 512)].rearrange("(k p) m -> p k m", p=P))

            def load_attention(x, kc, vc, f_scr):
                def keys(b):
                    sp.dma_start(Knat, kc[b].rearrange("(k p) c -> p k c", p=P)).then_inc(sem("k_in" + x), 16)

                def values(b):
                    sp.dma_start(Vc, vc[b].rearrange("(k p) c -> p k c", p=P)).then_inc(sem("v_in" + x), 16)

                def forget(b):
                    if f_scr is not None:
                        for hg in range(2):
                            src = f_scr[bass.ds(b * HB + hg * 8, 8), :].rearrange("h (o n) -> h o n", o=1)
                            sp.dma_start(FS[:, hg, :], src.to_broadcast([8, DS, T])).then_inc(sem("f_in" + x), 16)

                def rows(p):
                    if f_scr is not None:
                        for c in range(2):
                            sp.dma_start(FP[:, c, :], f_prompt_scr[bass.ds(p * 2 + c, 1), :].to_broadcast([P, NP])).then_inc(
                                sem("row_in"), 16)

                if x == "A":
                    sp.wait_ge(sem("ht_readyA"), 32)
                    keys(0)
                    sp.dma_start(own, new_mask).then_inc(sem("own_in"), 16)
                    sp.wait_ge(sem("ak_stored"), 32)
                else:
                    sp.wait_ge(sem("qT_copied"), 1)
                    keys(0)
                rows(0)
                forget(0)
                values(0)

                def following(b, more):
                    if f_scr is not None:
                        sp.wait_ge(sem("biased" + x), b * 2)
                        forget(b)
                    if more:
                        sp.wait_ge(sem("kt_ready" + x), b * 8 + 8)
                        keys(b + 1)
                    if f_scr is not None:
                        sp.wait_ge(sem("rows_free"), b)
                        rows(b)
                    sp.wait_ge(sem("pv_ready" + x), b * 2)
                    values(b)

                sp.wait_ge(sem("kt_ready" + x), 8)
                keys(1)
                with sp.Fori(1, DB - 1) as b:
                    following(b, True)
                following(DB - 1, False)
                sp.wait_ge(sem("o_ready" + x), primed(PAIR))

            load_ffn(0, BASE["ffn0"])
            load_rows(w_qkv_a[0], BASE["qkv"], 6)
            load_attention("A", cache_a_k[0].rearrange("b t h c d -> b t (h c d)"),
                       cache_a_v[0].rearrange("b t h e -> b t (h e)"), None)
            load_square(w_o_a[0], BASE["oa"])
            load_ffn(1, BASE["ffn1"])
            load_rows(w_kv_b, BASE["kv"], 4)
            s = BASE["wf"] % 2
            tile(BASE["wf"], s, raw[s][:, 0:1024].rearrange("p (k m) -> p k m", k=KB)[:, :, 0:HB],
                 w_f_b.rearrange("(k p) h -> p k h", p=P))
            sp.wait_ge(w_used, BASE["kv"])
            for k in range(PB):
                sp.dma_start(LN[:, k, :].rearrange("p (b h) -> p b h", b=DB),
                             cache_b_logf[:, k * P:(k + 1) * P, :].rearrange("b p h -> p b h")).then_inc(sem("logf_in"), 16)
            load_ffn(2, BASE["ffn2"])
            load_square(w_q_b[0], BASE["qb"])
            load_attention("B", cache_b_k.rearrange("b t h d -> b t (h d)"), cache_b_v.rearrange("b t h d -> b t (h d)"),
                       f_sample_scr)
            load_square(w_o_b[0], BASE["ob"])
            load_ffn(3, BASE["ffn3"])

        @block.gpsimd
        def _(pool):
            def split(n, slot, words, landed):
                pool.wait_ge(w_loaded[slot], landed)
                if not isinstance(n, int) or n >= 2:
                    pool.wait_ge(w_used, n - 1)
                pool.sem_inc(sem("pool_passed"), 1)
                pool.tensor_copy(w_hi[slot][:, 0:words], raw[slot][:, 0:words]).then_inc(w_hi_made, 1)
                pool.wait_ge(w_hi_made, n + 1)
                pool.tensor_tensor(w_lo[slot][:, 0:words], raw[slot][:, 0:words],
                                   w_hi[slot][:, 0:words].bitcast(F32), ALU.subtract).then_inc(w_split, 1)

            def run(base, count, words):
                first = 0
                if base == 0:
                    split(0, 0, words, 16)
                    split(1, 1, words, 16)
                    first = 1
                with pool.Fori(first, count // 2) as i:
                    for u in range(2):
                        s = (base + u) % 2
                        split(base + i * 2 + u, s, words, i * 16 + 16 * ((base + u) // 2 + 1))

            def run_ffn(base):
                for g in range(GRP):
                    run(base, 2 * FB, KB * P)
                    run(base + 2 * FB, KB, FB * P)
                    base += 2 * FB + KB

            run_ffn(BASE["ffn0"])
            run(BASE["qkv"], QKV_TILES, 1024)
            run(BASE["oa"], SQ_TILES, 1024)
            run_ffn(BASE["ffn1"])
            run(BASE["kv"], KV_TILES, 1024)
            n = BASE["wf"]
            split(n, n % 2, 1024, 16 * (n // 2 + 1))
            run_ffn(BASE["ffn2"])
            run(BASE["qb"], SQ_TILES, 1024)
            run(BASE["ob"], SQ_TILES, 1024)
            run_ffn(BASE["ffn3"])

        @block.tensor
        def _(pe):
            def flip(dst, src, rows=P):
                return pe.transpose(dst, src, cst[0:rows, IDENT:IDENT + rows])

            def stationary_tile(slot, kb, x_hi, x_lo, out, ready=None):
                for k in range(kb):
                    if ready is not None and ready(k) is not None:
                        pe.wait_ge(*ready(k))
                    w = slice(k * P, (k + 1) * P)
                    for a, x in ((w_hi, x_hi), (w_hi, x_lo), (w_lo, x_hi)):
                        for h in range(2):
                            last = pe.matmul(out[:, h, :], a[slot][:, w], x[:, k, h * HT:(h + 1) * HT],
                                             start=(k == 0 and a is w_hi and x is x_hi),
                                             stop=(k == kb - 1 and a is w_lo))
                last.then_inc(w_used, 1)
                return last

            def stats(n):
                pe.wait_ge(sem("squares_summed"), n + 1)
                for h in range(2):
                    last = pe.matmul(pair(0)[:, h, :], ones_d[:, :], sqacc[:, h * HT:(h + 1) * HT], start=True, stop=True)
                last.then_inc(sem("mean_ready"), 1)

            def ffn(f, base, norm):
                for g in range(GRP):
                    at = base + g * (2 * FB + KB)

                    def hidden(i, first, count):
                        s = at % 2
                        blk = count + i
                        pe.wait_ge(w_split, at + i * 2 + 1)
                        if not isinstance(blk, int) or blk >= 1:
                            pe.wait_ge(sem("gate_read"), blk)
                        stationary_tile(s, KB, xn_hi, xn_lo, pair(0),
                                        (lambda k: (sem("xn_ready"), primed(norm * KB + k + 1))) if first else None)
                        pe.wait_ge(w_split, at + i * 2 + 2)
                        if not isinstance(blk, int) or blk >= 1:
                            pe.wait_ge(sem("up_read"), primed(blk))
                        stationary_tile(1 - s, KB, xn_hi, xn_lo, pair(1))

                    count = (f * GRP + g) * FB
                    hidden(0, g == 0, count)
                    with pe.Fori(1, FB) as i:
                        hidden(i, False, count)
                    at += 2 * FB
                    ready = (f * GRP + g) * FB
                    pe.wait_ge(sem("act_ready"), primed(ready + FB - 2))
                    down(at, FB, act_hi, act_lo, lambda k: (sem("act_ready"), primed(ready + FB)) if k == FB - 2 else None)

            rounds = [0]

            def down(at, kb, hi, lo, ready=None):
                done = rounds[0] * KB
                rounds[0] += 1
                with pe.Fori(0, KB // 2) as m:
                    for u in range(2):
                        pe.wait_ge(w_split, at + m * 2 + u + 1)
                        pe.wait_ge(sem("down_read"), done + m * 2 + u + 1)
                        stationary_tile((at + u) % 2, kb, hi, lo, pair(2 + u), ready)

            def token_tile(at, done, n, norm):
                for u in range(4):
                    s = (at + u) % 2
                    pe.wait_ge(w_split, n * 4 + (at + u + 1))
                    for kk in range(2):
                        k = 2 * u + kk
                        pe.wait_ge(sem("xn_ready"), primed(norm * KB + k + 1))
                        for t in range(TB):
                            if k == 0:
                                pe.wait_ge(sem("rows_read"), n * TB + (done * TB + t + 1))
                            cols = slice(t * P, (t + 1) * P)
                            w = slice(kk * 512, (kk + 1) * 512)
                            for x, a in ((xn_hi, w_hi), (xn_hi, w_lo), (xn_lo, w_hi)):
                                last = pe.matmul(PS[:, t, :], x[:, k, cols], a[s][:, w],
                                                 start=(k == 0 and x is xn_hi and a is w_hi), stop=(k == KB - 1 and x is xn_lo))
                    last.then_inc(w_used, 1)

            def head_transposes(x, src, parts):
                for w in range(parts):
                    for h in range(PAIR):
                        for g, blocks in enumerate((range(0, 4), range(4, 5))):
                            n = (w * PAIR + h) * 2 + g
                            bank = n % 4
                            if n >= 4:
                                pe.wait_ge(sem(("ht_act" if n % 2 else "ht_dve") + x), (n - 4) // 2 + 1)
                            for j, t in enumerate(blocks):
                                last = flip(PS[:, bank, j * P:(j + 1) * P], src[:, w, t, h * P:(h + 1) * P])
                            last.then_inc(sem("ht_ready" + x), 1)

            def attend(x):
                mask = cst[:, CHUNKED:CHUNKED + P] if x == "A" else cst[:, CAUSAL:CAUSAL + P]
                parts = range(1 if x == "A" else 2)

                def scores(h, t):
                    if t == 0:
                        pe.wait_ge(sem("qk_staged" + x), h + 1)
                        if not isinstance(h, int) or h > 0:
                            pe.wait_ge(sem("pt_read" + x), h * 4)
                    else:
                        pe.wait_ge(sem("pt_read" + x), h * 4 + t)
                    for c in range(2):
                        rows = slice(64 * c, 64 * c + 64)
                        pe.matmul(PS[:, c, 0:(t + 1) * P], qh[rows, t * P:(t + 1) * P], kh[rows, 0:(t + 1) * P],
                                  start=True, stop=False)
                        last = pe.matmul(PS[:, c, t * P:(t + 1) * P], ident, mask, start=False, stop=True)
                    last.then_inc(sem("s_ready" + x), 1)

                def turn(h, t):
                    pe.wait_ge(sem("p_ready" + x), h * 4 + t + 1)
                    for c in parts:
                        for k in range(t + 1):
                            last = flip(PS[:, c, k * P:(k + 1) * P], PR[:, c, k * P:(k + 1) * P])
                    last.then_inc(sem("pt_ready" + x), 1)

                def output(h, following):
                    if following:
                        pe.wait_ge(sem("kt_act" + x), h * 4 + 8)
                    pe.wait_ge(sem("pt_read" + x), h * 4 + 4)
                    pe.wait_ge(sem("v_staged" + x), h + 1)
                    for c in parts:
                        e = slice(0, P) if x == "A" else slice(64 * c, 64 * c + 64)
                        for k in range(PB):
                            last = pe.matmul(PS[e, 6, k * P:512], vh[:, k, e], pT[:, c, k, k * P:512],
                                             start=(k == 0), stop=(k == PB - 1), skip_group_check=True)
                    last.then_inc(sem("o_ready" + x), 1)

                def turn_keys(b, heads):
                    for h in heads:
                        if h == 0:
                            pe.wait_ge(sem("k_in" + x), b * 16 + 16)
                            if not isinstance(b, int) or b > 0:
                                pe.wait_ge(sem("o_read" + x), primed(b - 1))
                        if h >= 2:
                            pe.wait_ge(sem(("kt_dve" if h % 2 else "kt_act") + x), b * 4 + (h - 2) // 2 + 1)
                        for k in range(PB):
                            last = flip(PS[:, 6 + h % 2, k * P:(k + 1) * P], Knat[:, k, h * P:(h + 1) * P])
                        last.then_inc(sem("kt_ready" + x), 1)

                def stream_scores(b):
                    pe.wait_ge(sem("kt_dve" + x), b * 4 + 4)
                    pe.wait_ge(sem("kt_act" + x), b * 4 + 4)
                    pe.wait_ge(sem("q_staged" + x), b + 1)
                    pe.wait_ge(sem("oT_read" + x), primed(b * 2))
                    for g in range(2):
                        new = PS[:, 3 + 2 * g, 0:P]
                        for j in range(4):
                            h, rows = 4 * g + j, slice(32 * j, 32 * j + 32)
                            pe.matmul(PS[rows, 2 + 2 * g, :], qbd[:, h, :], kTc[:, h, :], start=True, stop=True,
                                      tile_position=(0, 32 * j), skip_group_check=True)
                            pe.matmul(new[rows], qbd[:, h, :], kT[:, h, NP:T], start=True, stop=False,
                                      tile_position=(0, 32 * j), skip_group_check=True)
                        if x == "A":
                            last = pe.matmul(new, ones_e[0:1, :], own[0:1, bass.ds(b * P, P)], start=False, stop=True,
                                             skip_group_check=True)
                        else:
                            last = pe.matmul(new, cst[0:DS, QSEL:QSEL + P], cst[0:DS, QTRI:QTRI + P],
                                             start=False, stop=True, skip_group_check=True)
                        last.then_inc(sem("ss_ready" + x), 1)

                def stream_turn(b, g):
                    pe.wait_ge(sem("norm_ready" + x), b * 2 + g + 1)
                    for k in range(PB + 1):
                        last = pe.matmul(wide(2 + 2 * g)[:, k * P:(k + 1) * P], (t0, t1)[g][:, k * P:(k + 1) * P],
                                         Cm[:, g, :], start=True, stop=True)
                    last.then_inc(sem("pd_ready" + x), 1)

                def stream_values(b, g, blocks):
                    if g == 0:
                        pe.wait_ge(sem("v_in" + x), b * 16 + 16)
                    pe.wait_ge(sem("pd_read" + x + str(g)), b + 1)
                    for k in blocks:
                        v = Vc[:, k, g * 512:(g + 1) * 512] if k < PB else vN[:, TB - 1, g * 512:(g + 1) * 512]
                        last = pe.matmul(PS[:, 2 + 2 * g, :], (t2, sqacc)[g][:, k * P:(k + 1) * P], v,
                                         start=(k == 0), stop=(k == PB), skip_group_check=True)
                    if k == PB:
                        last.then_inc(sem("pv_ready" + x), 1)

                def stream_output(b, g):
                    pe.wait_ge(sem("oN_ready" + x + str(g)), b + 1)
                    flip(PS[:, 3 + 2 * g, 0:P], oN[:, g, :]).then_inc(sem("oT_ready" + x), 1)

                def round_(i, following):
                    stream_scores(i)
                    turn(i, 0)
                    if following:
                        turn_keys(i + 1, range(0, 2))
                    scores(i, 1)
                    if following:
                        turn_keys(i + 1, range(2, 8))
                    turn(i, 1)
                    stream_turn(i, 0)
                    stream_turn(i, 1)
                    scores(i, 2)
                    stream_values(i, 0, range(0, PB))
                    turn(i, 2)
                    stream_values(i, 0, range(PB, PB + 1))
                    scores(i, 3)
                    stream_output(i, 0)
                    stream_values(i, 1, range(0, PB))
                    turn(i, 3)
                    stream_values(i, 1, range(PB, PB + 1))
                    if following:
                        scores(i + 1, 0)
                    stream_output(i, 1)
                    output(i, following)

                turn_keys(0, range(8))
                scores(0, 0)
                with pe.Fori(0, PAIR - 1) as i:
                    round_(i, True)
                round_(PAIR - 1, False)
                pe.wait_ge(sem("o_read" + x), primed(PAIR))

            pe.sem_inc(sem("o_readyA"), 1)
            pe.sem_inc(sem("o_readyB"), 1)
            pe.wait_ge(setup_in, 16 * 9)
            flip(PS[:, 7, 0:65], gN[0:65, :], 65).then_inc(sem("g_turned"), 1)
            for k in range(KB):
                for g, blocks in enumerate((range(0, 4), range(4, 5))):
                    n = 2 * k + g
                    if n >= 4:
                        pe.wait_ge(sem("x_evac_dve" if g else "x_evac_act"), k - 1)
                    for j, t in enumerate(blocks):
                        last = flip(PS[:, n % 4, j * P:(j + 1) * P], xN[:, t, k * P:(k + 1) * P])
                    last.then_inc(sem("x_turned"), 1)
            pe.wait_ge(sem("x_evac_act"), KB)
            pe.wait_ge(sem("x_evac_dve"), KB)
            pe.wait_ge(sem("ones_made"), 3)
            stats(0)
            ffn(0, BASE["ffn0"], 0)
            stats(1)
            with pe.Fori(0, 6) as n:
                token_tile(BASE["qkv"], 0, n, 1)
            pe.wait_ge(sem("rope_done"), 2)
            pe.wait_ge(sem("rows_read"), 7 * TB)
            head_transposes("A", nat, 2)
            pe.wait_ge(sem("ht_actA"), 16)
            pe.wait_ge(sem("ht_dveA"), 16)
            pe.wait_ge(sem("own_in"), 16)
            attend("A")
            with pe.Fori(0, PAIR // 2) as i:
                for u in range(2):
                    pe.wait_ge(sem("o_squared"), i * 2 + u + 1)
                    for h in range(2):
                        last = pe.matmul(pair(u)[:, h, :], ones_e[:, :], (sqacc, t2)[u][:, h * HT:(h + 1) * HT], start=True, stop=True)
                    last.then_inc(sem("o_mean"), 1)
            down(BASE["oa"], KB, xn_hi, xn_lo, lambda k: (sem("oA_split"), k + 1))
            stats(2)
            ffn(1, BASE["ffn1"], 2)
            stats(3)
            with pe.Fori(0, 4) as n:
                token_tile(BASE["kv"], 6, n, 3)
            pe.wait_ge(w_split, BASE["wf"] + 1)
            stationary_tile(BASE["wf"] % 2, KB, xn_hi, xn_lo, pair(3))
            pe.wait_ge(sem("rows_read"), 11 * TB)
            head_transposes("B", nat, 1)
            pe.wait_ge(sem("logf_in"), 64)
            pe.wait_ge(sem("ht_actB"), 8)
            pe.wait_ge(sem("ht_dveB"), 8)
            for k in range(PB):
                last = flip(PS[:, 1, k * P:(k + 1) * P], LN[:, k, :])
            last.then_inc(sem("LT_ready"), 1)
            pe.wait_ge(sem("logf_done"), 1)
            for t in range(TB):
                last = flip(PS[:, 2, t * HB:(t + 1) * HB], lfT[:, t * P:(t + 1) * P], HB)
            last.then_inc(sem("lfN_ready"), 1)
            pe.wait_ge(sem("EX_done"), 1)
            pe.matmul(PS[:, 3, 0:DS], EX, cst[:, STEP:STEP + DS], start=True, stop=True).then_inc(sem("new_ready"), 1)
            pe.wait_ge(sem("new_read"), 1)
            ffn(2, BASE["ffn2"], 4)
            stats(4)
            down(BASE["qb"], KB, xn_hi, xn_lo, lambda k: (sem("xn_ready"), primed(5 * KB + k + 1)))
            pe.wait_ge(sem("qT_copied"), 1)
            attend("B")
            down(BASE["ob"], KB, xn_hi, xn_lo, lambda k: (sem("oB_split"), k + 1))
            stats(5)
            ffn(3, BASE["ffn3"], 6)
            stats(6)
            for k in range(KB):
                pe.wait_ge(sem("y_ready"), k + 1)
                for g, blocks in enumerate((range(0, 4), range(4, 5))):
                    n = 2 * k + g
                    if n >= 4:
                        pe.wait_ge(sem("y_evac_dve" if g else "y_evac_act"), k - 1)
                    for j, t in enumerate(blocks):
                        last = flip(PS[:, 4 + n % 4, j * P:(j + 1) * P], yT[:, k, t * P:(t + 1) * P])
                    last.then_inc(sem("y_turned"), 1)

        @block.scalar
        def _(act):
            step = sem("act_step")
            count = Count()

            def norm(stat, n):
                if stat is not None:
                    act.wait_ge(sem("mean_ready"), stat + 1)
                    act.activation(halves(t0[:, :]), pair(0), ACT.Ln, bias=eps).then_inc(step, 1)
                    act.wait_ge(step, count.next())
                    act.activation(t1[:, :], t0[:, :], ACT.Exp, scale=-0.5).then_inc(sem("root_ready"), 1)
                if n == 7:
                    return
                with act.Fori(0, KB // 2) as i:
                    for u in range(2):
                        act.wait_ge(sem("scaled"), n * KB + i * 2 + u + 1)
                        act.activation(xn_hi[:, i * 2 + u, :], oT[:, i * 2 + u, :], ACT.Copy).then_inc(
                            sem("hi_ready"), 1)

            def ffn(f, base):
                for g in range(GRP):
                    at, blk = base + g * (2 * FB + KB), (f * GRP + g) * FB
                    with act.Fori(0, FB) as i:
                        act.wait_ge(w_used, at + i * 2 + 1)
                        act.wait_ge(sem("up_read"), primed(blk + i))
                        act.activation(halves(t0[:, :]), pair(0), ACT.Silu).then_inc(sem("gate_read"), 1)

            def heads(x, parts):
                for w in range(parts):
                    dst = (qT, kT)[w] if parts == 2 else kT
                    for h in range(PAIR):
                        act.wait_ge(sem("ht_ready" + x), (w * PAIR + h) * 2 + 2)
                        act.activation(dst[:, h, NP:T], PS[:, (2 * h + 1) % 4, 0:P], ACT.Copy).then_inc(sem("ht_act" + x), 1)

            def attend(x):
                parts = range(1 if x == "A" else 2)

                def stage_queries(h):
                    act.activation(qh, qT[:, h, 0:NP], ACT.Copy)
                    act.activation(kh, kT[:, h, 0:NP], ACT.Copy).then_inc(sem("qk_staged" + x), 1)

                def stage_values(h, at):
                    act.wait_ge(sem("o_ready" + x), primed(h))
                    act.activation(vh, vN[:, 0:PB, at], ACT.Copy).then_inc(sem("v_staged" + x), 1)

                def exps(h, t):
                    n = (t + 1) * P
                    act.wait_ge(sem("nb_ready" + x), h * 4 + t + 1)
                    for c in range(2):
                        src = PS[:, c, 0:n] if x == "A" else PR[:, c, 0:n]
                        last = act.activation(PR[:, c, 0:n], src, ACT.Exp, bias=st[:, 0, 2 + c:3 + c],
                                              scale=SCALE if x == "A" else 1.0, accum_out=st[:, 0, 4 + c:5 + c])
                    last.then_inc(sem("exp_done" + x), 1)

                def turned(h, t):
                    act.wait_ge(sem("pt_ready" + x), h * 4 + t + 1)
                    for c in parts:
                        last = act.activation(pT[:, c, 0:t + 1, t * P:(t + 1) * P],
                                              PS[:, c, 0:(t + 1) * P].rearrange("p (k q) -> p k q", q=P), ACT.Copy)
                    last.then_inc(sem("pt_read" + x), 1)

                def stage(b):
                    at = bass.ds(b * DS + NP, DS)
                    act.activation(qbd[0:64, :, 0:DS], qT[0:64, :, at], ACT.Copy)
                    act.activation(qbd[64:P, :, DS:2 * DS], qT[64:P, :, at], ACT.Copy).then_inc(sem("q_staged" + x), 1)

                def keys(b, heads):
                    for h in heads:
                        act.wait_ge(sem("kt_ready" + x), b * 8 + h + 1)
                        act.activation(kTc[:, h, :], PS[:, 6 + h % 2, :], ACT.Copy).then_inc(sem("kt_act" + x), 1)

                def stream_exps(b):
                    for g in range(2):
                        act.wait_ge(sem("snb_ready" + x), b * 2 + g + 1)
                        p = (t0, t1)[g][:, :]
                        act.activation(p, wide(2 + 2 * g) if x == "A" else p, ACT.Exp, bias=st[:, 1 + g, 2:3],
                                       scale=SCALE if x == "A" else 1.0,
                                       accum_out=st[:, 1 + g, 4:5]).then_inc(sem("sexp_done" + x), 1)

                def round_(i, following):
                    exps(i, 0)
                    turned(i, 0)
                    stage_values(i, bass.ds(i * P, P) if following else slice(i * P, (i + 1) * P))
                    if following:
                        keys(i + 1, (0,))
                    stream_exps(i)
                    if following:
                        keys(i + 1, (2,))
                    exps(i, 1)
                    if following:
                        keys(i + 1, (4, 6))
                    turned(i, 1)
                    if following:
                        stage(i + 1)
                    act.wait_ge(sem("pd_ready" + x), i * 2 + 1)
                    act.activation(t2[:, :], wide(2), ACT.Copy).then_inc(sem("pd_read" + x + "0"), 1)
                    exps(i, 2)
                    turned(i, 2)
                    act.wait_ge(sem("pv_ready" + x), i * 2 + 1)
                    for j in range(4):
                        rows = slice(32 * j, 32 * j + 32)
                        last = act.activation(oN[rows, 0, :], PS[rows, 2, j * P:(j + 1) * P], ACT.Copy)
                    last.then_inc(sem("oN_ready" + x + "0"), 1)
                    exps(i, 3)
                    if following:
                        stage_queries(i + 1)
                    turned(i, 3)

                stage_queries(0)
                act.wait_ge(sem("qbd_clear" + x), 1)
                stage(0)
                keys(0, (0, 2, 4, 6))
                with act.Fori(0, PAIR - 1) as i:
                    round_(i, True)
                round_(PAIR - 1, False)

            act.wait_ge(sem("lam_sums"), 1)
            act.activation(small[:, 4:6], small[:, 6:8], ACT.Exp).then_inc(sem("lam_exps"), 1)
            eps = small[:, 10:11]
            for k in range(KB):
                act.wait_ge(sem("x_turned"), 2 * k + 1)
                act.activation(xT[:, k, 0:NP], PS[:, (2 * k) % 4, :], ACT.Copy).then_inc(sem("x_evac_act"), 1)
            norm(0, 0)
            ffn(0, BASE["ffn0"])
            norm(1, 1)
            act.wait_ge(sem("rope_done"), 2)
            rows = "l b (t p) h c d -> p (l b t) (h c d)"
            act.dma_start(ak_prompt.rearrange(rows, p=P), nat[:, 1, 0:4, :]).then_inc(sem("ak_stored"), 16)
            act.dma_start(ak_sample.rearrange("l b t h c d -> (l b t) (h c d)"), nat[:, 1, 4, :]).then_inc(sem("ak_stored"), 16)
            act.wait_ge(sem("rows_read"), 7 * TB)
            act.dma_start(av_prompt.rearrange("l b (t p) h e -> p (l b t) (h e)", p=P), vN[:, 0:4, :]).then_inc(sem("av_stored"), 16)
            act.dma_start(av_sample.rearrange("l b t h e -> (l b t) (h e)"), vN[:, 4, :]).then_inc(sem("av_stored"), 16)
            heads("A", 2)
            act.wait_ge(sem("ak_stored"), 32)
            attend("A")
            with act.Fori(0, PAIR // 2) as i, count.loop(i, PAIR // 2, 2):
                for u in range(2):
                    act.wait_ge(sem("o_mean"), i * 2 + u + 1)
                    act.wait_ge(sem("o_scaled"), i * 2 + u + 1)
                    act.activation(halves((t0, t1)[u][:, :]), pair(u), ACT.Ln, bias=eps).then_inc(step, 1)
                    count.next()
                for u in range(2):
                    act.wait_ge(step, count.off + (count.n - 1 + u))
                    act.activation((t0, t1)[u][:, :], (t0, t1)[u][:, :], ACT.Exp, scale=-0.5).then_inc(sem("o_root"), 1)
                for u in range(2):
                    act.wait_ge(sem("o_scaled"), i * 2 + u + 3)
                    act.activation(xn_hi[:, i * 2 + u, :], oT[:, i * 2 + u, :], ACT.Copy).then_inc(sem("oA_hi"), 1)
            norm(2, 2)
            ffn(1, BASE["ffn1"])
            norm(3, 3)
            act.wait_ge(sem("rows_read"), 9 * TB)
            act.dma_start(bk_prompt.rearrange("b (t p) h d -> p (b t) (h d)", p=P), nat[:, 0, 0:4, :]).then_inc(sem("bk_stored"), 16)
            act.dma_start(bk_sample.rearrange("b t h d -> (b t) (h d)"), nat[:, 0, 4, :]).then_inc(sem("bk_stored"), 16)
            act.wait_ge(sem("rows_read"), 11 * TB)
            act.dma_start(bv_prompt.rearrange("b (t p) h d -> p (b t) (h d)", p=P), vN[:, 0:4, :]).then_inc(sem("bv_stored"), 16)
            act.dma_start(bv_sample.rearrange("b t h d -> (b t) (h d)"), vN[:, 4, :]).then_inc(sem("bv_stored"), 16)
            act.wait_ge(sem("absz_ready"), 1)
            act.activation(lf2, lf1, ACT.Exp, scale=-1.0).then_inc(step, 1)
            act.wait_ge(step, count.next())
            act.activation(lf1, lf2, ACT.Ln, bias=1.0).then_inc(sem("ln_ready"), 1)
            heads("B", 1)
            act.wait_ge(sem("lfN_read"), 1)
            act.dma_start(bf_prompt.rearrange("b (t p) h -> p (b t) h", p=P), lfN[:, 0:4, :]).then_inc(sem("bf_stored"), 16)
            act.dma_start(bf_sample.rearrange("b t h -> (b t) h"), lfN[:, 4, :]).then_inc(sem("bf_stored"), 16)
            act.dma_start(f_prompt_scr, FCp).then_inc(sem("bf_stored"), 16)
            act.wait_ge(sem("LO_ready"), 1)
            act.dma_start(f_sample_scr, LO).then_inc(sem("bf_stored"), 16)
            norm(None, 4)
            ffn(2, BASE["ffn2"])
            norm(4, 5)
            act.wait_ge(sem("qT_copied"), 1)
            attend("B")
            with act.Fori(0, PAIR) as h:
                act.wait_ge(sem("oT_readB"), primed(2 * DB))
                act.wait_ge(sem("o_readB"), primed(PAIR))
                act.activation(xn_hi[:, h, :], oT[:, h, :], ACT.Copy).then_inc(sem("oB_hi"), 1)
            norm(5, 6)
            ffn(3, BASE["ffn3"])
            norm(6, 7)
            for k in range(KB):
                act.wait_ge(sem("y_turned"), 2 * k + 1)
                src = PS[:, 4 + (2 * k) % 4, :].rearrange("p (t c) -> p t c", c=P)
                act.activation(yN[:, 0:4, k * P:(k + 1) * P], src, ACT.Copy).then_inc(sem("y_evac_act"), 1)
                if k % 4 == 3:
                    half = slice((k - 3) * P, (k + 1) * P)
                    act.wait_ge(sem("y_evac_act"), k + 1)
                    act.wait_ge(sem("y_evac_dve"), k + 1)
                    act.dma_start(y_prompt[0][:, half].rearrange("(t p) d -> p t d", p=P), yN[:, 0:4, half]).then_inc(
                        sem("y_stored"), 16)
                    act.dma_start(y_sample[:, :, half].rearrange("b t d -> (b t) d"), yN[:, 4, half]).then_inc(
                        sem("y_stored"), 16)
            for name, n in (("ak_stored", 2), ("av_stored", 2), ("bk_stored", 2), ("bv_stored", 2), ("bf_stored", 4), ("y_stored", 4)):
                act.wait_ge(sem(name), 16 * n)

        @block.vector
        def _(dve):
            step = sem("dve_step")
            count = Count()

            def norm(stat, n, g):
                if stat is not None:
                    dve.wait_ge(sem("root_ready"), stat + 1)

                def scale(i):
                    for u in range(2):
                        k = i * 2 + u
                        dve.scalar_tensor_tensor(out=oT[:, k, :], in0=xT[:, k, :],
                                                 scalar=gT[:, bass.ds(k + 8 * g, 1)], in1=t1[:, :], op0=ALU.mult,
                                                 op1=ALU.mult).then_inc(sem("scaled"), 1)

                def rest(i):
                    for u in range(2):
                        k = i * 2 + u
                        dve.wait_ge(sem("hi_ready"), n * KB + k + 1)
                        dve.tensor_tensor(xn_lo[:, k, :], oT[:, k, :], xn_hi[:, k, :].bitcast(F32),
                                          ALU.subtract).then_inc(sem("xn_ready"), 1)

                scale(0)
                with dve.Fori(0, KB // 2 - 1) as i:
                    scale(i + 1)
                    rest(i)
                rest(KB // 2 - 1)
                dve.wait_ge(sem("xn_ready"), primed((n + 1) * KB))

            def add_square(x):
                dve.tensor_tensor(t2[:, :], x, x, ALU.mult).then_inc(step, 1)
                dve.wait_ge(step, count.next())
                dve.tensor_tensor(sqacc[:, :], sqacc[:, :], t2[:, :], ALU.add).then_inc(step, 1)
                dve.wait_ge(step, count.next())

            def clear_squares():
                dve.memset(sqacc[:, :], 0.0).then_inc(step, 1)
                dve.wait_ge(step, count.next())

            def add_down(at, factor, squares):
                if squares:
                    clear_squares()
                with dve.Fori(0, KB // 2) as m, count.loop(m, KB // 2, 4 if squares else 0):
                    for u in range(2):
                        dve.wait_ge(w_used, at + m * 2 + u + 1)
                        x = xT[:, m * 2 + u, :]
                        dve.scalar_tensor_tensor(out=halves(x), in0=pair(2 + u), scalar=factor, in1=halves(x),
                                                 op0=ALU.mult, op1=ALU.add).then_inc(sem("down_read"), 1)
                        dve.wait_ge(sem("down_read"), sums[0] + m * 2 + u + 3)
                        if squares:
                            add_square(x)
                sums[0] += KB
                if squares:
                    dve.sem_inc(sem("squares_summed"), 1)

            sums = [0]

            def ffn(f, base):
                for g in range(GRP):
                    at, blk = base + g * (2 * FB + KB), (f * GRP + g) * FB
                    with dve.Fori(0, FB) as i, count.loop(i, FB, 1):
                        dve.wait_ge(w_used, at + i * 2 + 2)
                        dve.wait_ge(sem("gate_read"), blk + i + 1)
                        dve.wait_ge(sem("act_ready"), primed(blk + i))
                        dve.tensor_tensor(halves(t1[:, :]), halves(t0[:, :]), pair(1), ALU.mult).then_inc(sem("up_read"), 1)
                        dve.wait_ge(sem("up_read"), primed(blk + i + 1))
                        dve.tensor_copy(act_hi[:, i, :], t1[:, :]).then_inc(step, 1)
                        dve.wait_ge(step, count.next())
                        dve.tensor_tensor(act_lo[:, i, :], t1[:, :], act_hi[:, i, :].bitcast(F32),
                                          ALU.subtract).then_inc(sem("act_ready"), 1)
                    add_down(at + 2 * FB, 0.5, g == GRP - 1)

            def rows_out(dst, at, n0, tiles):
                with dve.Fori(0, tiles) as n:
                    dve.wait_ge(w_used, n * 4 + (at + 4 * n0 + 4))
                    for t in range(TB):
                        dve.tensor_copy(dst[:, t, bass.ds(n * 512, 512)], PS[:, t, :]).then_inc(sem("rows_read"), 1)

            def rope(x):
                v = x.rearrange("p t (m d) -> p t m d", d=64)
                x1, x2 = v[:, :, :, 0:8], v[:, :, :, 8:16]
                shape = [P, TB, 16, 8]
                cos = rope_consts[:, :, 0:8].rearrange("p t (o d) -> p t o d", o=1).to_broadcast(shape)
                sin = rope_consts[:, :, 8:16].rearrange("p t (o d) -> p t o d", o=1).to_broadcast(shape)
                tmp = [t[:, :].rearrange("p (t m d) -> p t m d", t=TB, d=8) for t in (t0, t1, t2, sqacc)]
                for out, a, b in zip(tmp, (x1, x2, x2, x1), (cos, sin, cos, sin)):
                    dve.tensor_tensor(out, a, b, ALU.mult).then_inc(step, 1)
                    seen = count.next()
                dve.wait_ge(step, seen)
                dve.tensor_tensor(x1, tmp[0], tmp[1], ALU.subtract)
                dve.tensor_tensor(x2, tmp[2], tmp[3], ALU.add).then_inc(sem("rope_done"), 1)

            def heads(x, parts):
                for w in range(parts):
                    dst = (qT, kT)[w] if parts == 2 else kT
                    for h in range(PAIR):
                        dve.wait_ge(sem("ht_ready" + x), (w * PAIR + h) * 2 + 1)
                        dve.tensor_copy(dst[:, h, 0:NP], PS[:, (2 * h) % 4, :]).then_inc(sem("ht_dve" + x), 1)

            def attend(x):
                s0 = st[:, 0, :]

                def peak(h, t):
                    n = (t + 1) * P
                    dve.wait_ge(sem("s_ready" + x), h * 4 + t + 1)
                    for c in range(2):
                        if x == "A":
                            last = dve.reduce_max(s0[:, c:c + 1], PS[:, c, 0:n], AX)
                        else:
                            if c == 0:
                                dve.sem_inc(sem("dve_passed"), 1)
                            last = dve.tensor_tensor_reduce(out=PR[:, c, 0:n], in0=PS[:, c, 0:n], in1=FP[:, c, 0:n],
                                                            scale=SCALE, scalar=-3e38, op0=ALU.add, op1=ALU.max,
                                                            accum_out=s0[:, c:c + 1])
                    last.then_inc(step, 1)
                    dve.wait_ge(step, count.next())
                    dve.tensor_scalar(s0[:, 2:4], s0[:, 0:2], -SCALE if x == "A" else -1.0, None, ALU.mult).then_inc(
                        sem("nb_ready" + x), 1)

                def combine(h, t):
                    n = (t + 1) * P
                    p0, p1 = PR[:, 0, 0:n], PR[:, 1, 0:n]
                    dve.wait_ge(sem("exp_done" + x), h * 4 + t + 1)
                    dve.reciprocal(s0[:, 4:6], s0[:, 4:6]).then_inc(step, 1)
                    dve.wait_ge(step, count.next())
                    if x == "A":
                        dve.tensor_tensor(s0[:, 5:6], s0[:, 5:6], neg_lam, ALU.mult).then_inc(step, 1)
                        dve.tensor_scalar(p0, p0, s0[:, 4:5], None, ALU.mult).then_inc(step, 1)
                        count.next()
                        dve.wait_ge(step, count.next())
                        dve.scalar_tensor_tensor(out=p0, in0=p1, scalar=s0[:, 5:6], in1=p0, op0=ALU.mult,
                                                 op1=ALU.add).then_inc(sem("p_readyA"), 1)
                    else:
                        dve.tensor_scalar(p0, p0, s0[:, 4:5], None, ALU.mult)
                        dve.tensor_scalar(p1, p1, s0[:, 5:6], None, ALU.mult).then_inc(sem("p_readyB"), 1)

                def keys(b, heads):
                    for h in heads:
                        dve.wait_ge(sem("kt_ready" + x), b * 8 + h + 1)
                        dve.tensor_copy(kTc[:, h, :], PS[:, 6 + h % 2, :]).then_inc(sem("kt_dve" + x), 1)

                def stream_peaks(b):
                    for g in range(2):
                        s = st[:, 1 + g, :]
                        dve.wait_ge(sem("ss_ready" + x), b * 2 + g + 1)
                        if x == "A":
                            dve.reduce_max(s[:, 0:1], wide(2 + 2 * g), AX).then_inc(step, 1)
                            dve.wait_ge(step, count.next())
                        else:
                            dve.wait_ge(sem("f_inB"), b * 32 + 32)
                            dve.sem_inc(sem("dve_passed"), 1)
                            dve.tensor_tensor_reduce(out=(t0, t1)[g][:, :], in0=wide(2 + 2 * g), in1=FS[:, g, :], scale=SCALE,
                                                     scalar=-3e38, op0=ALU.add, op1=ALU.max,
                                                     accum_out=s[:, 0:1]).then_inc(sem("biasedB"), 1)
                            dve.wait_ge(sem("biasedB"), b * 2 + g + 1)
                        dve.tensor_scalar(s[:, 2:3], s[:, 0:1], -SCALE if x == "A" else -1.0, None, ALU.mult).then_inc(
                            sem("snb_ready" + x), 1)

                def stream_norms(b):
                    for g in range(2):
                        s = st[:, 1 + g, :]
                        dve.wait_ge(sem("sexp_done" + x), b * 2 + g + 1)
                        dve.reciprocal(s[:, 5:6], s[:, 4:5]).then_inc(step, 1)
                        dve.wait_ge(step, count.next())
                        if x == "A":
                            dve.tensor_scalar(Cm[:, g, :], cst[:, SPREAD:SPREAD + P], s[:, 5:6], comp, ALU.mult,
                                              ALU.mult).then_inc(sem("norm_readyA"), 1)
                        else:
                            dve.tensor_scalar(Cm[:, g, :], ident, s[:, 5:6], None, ALU.mult).then_inc(sem("norm_readyB"), 1)

                def stream_output(b, g):
                    dve.wait_ge(sem("oT_ready" + x), b * 2 + g + 1)
                    src = PS[:, 3 + 2 * g, 0:P].rearrange("p (j c q) -> p j c q", j=4, c=2)
                    at = bass.ds(b * DS + NP, DS)
                    if x == "A":
                        last = dve.tensor_copy(oT[:, 4 * g:4 * g + 4, at], src[:, :, 0, :])
                    else:
                        for c in range(2):
                            e = slice(64 * c, 64 * c + 64)
                            last = dve.tensor_copy(oT[e, 4 * g:4 * g + 4, at], src[e, :, c, :])
                    last.then_inc(sem("oT_read" + x), 1)

                def first_peak(i):
                    if x == "B":
                        dve.wait_ge(sem("row_in"), i * 32 + 32)
                    peak(i, 0)

                def round_(i, following):
                    combine(i, 0)
                    stream_peaks(i)
                    if following:
                        keys(i + 1, (1,))
                    peak(i, 1)
                    if following:
                        keys(i + 1, (3,))
                    stream_norms(i)
                    if following:
                        keys(i + 1, (5,))
                    combine(i, 1)
                    if following:
                        keys(i + 1, (7,))
                    dve.wait_ge(sem("pd_ready" + x), i * 2 + 2)
                    dve.tensor_copy(sqacc[:, :], wide(4)).then_inc(sem("pd_read" + x + "1"), 1)
                    peak(i, 2)
                    combine(i, 2)
                    stream_output(i, 0)
                    peak(i, 3)
                    if x == "B":
                        dve.sem_inc(sem("rows_free"), 1)
                    combine(i, 3)
                    dve.wait_ge(sem("pv_ready" + x), i * 2 + 2)
                    for j in range(4):
                        rows = slice(32 * j, 32 * j + 32)
                        last = dve.tensor_copy(oN[rows, 1, :], PS[rows, 4, j * P:(j + 1) * P])
                    last.then_inc(sem("oN_ready" + x + "1"), 1)
                    if following:
                        first_peak(i + 1)
                    stream_output(i, 1)
                    dve.wait_ge(sem("o_ready" + x), primed(i + 1))
                    dve.tensor_copy(oT[:, i, 0:NP], PS[:, 6, :]).then_inc(sem("o_read" + x), 1)

                if x == "A":
                    dve.wait_ge(sem("ak_stored"), 32)
                dve.memset(qbd, 0.0).then_inc(sem("qbd_clear" + x), 1)
                keys(0, (1, 3, 5, 7))
                first_peak(0)
                per = 4 * (4 if x == "A" else 2) + (4 if x == "A" else 2)
                with dve.Fori(0, PAIR - 1) as i, count.loop(i, PAIR - 1, per):
                    round_(i, True)
                round_(PAIR - 1, False)

            dve.memset(ones_d[:, :], 1.0 / D).then_inc(sem("ones_made"), 1)
            dve.memset(ones_e[:, :], 1.0 / P).then_inc(sem("ones_made"), 1)
            dve.memset(small[:, 10:11], EPS).then_inc(sem("ones_made"), 1)
            for name in ("o_readA", "o_readB", "oT_readA", "oT_readB", "up_read", "xn_ready", "act_ready"):
                dve.sem_inc(sem(name), 1)
            dve.sem_inc(sem("down_read"), 2)
            dve.sem_inc(sem("o_scaled"), 2)
            dve.sem_inc(sem("rows_read"), TB)
            dve.wait_ge(setup_in, 16 * 9)
            for c in range(2):
                dve.tensor_tensor_reduce(out=t0[:, 64 * c:64 * c + 64], in0=lamN[:, 128 * c:128 * c + 64],
                                         in1=lamN[:, 128 * c + 64:128 * c + 128], scale=1.0, scalar=0.0, op0=ALU.mult,
                                         op1=ALU.add, accum_out=small[:, 6 + c:7 + c]).then_inc(sem("lam_sums" if c else "lam_sum0"), 1)
            clear_squares()
            for k in range(KB):
                dve.wait_ge(sem("x_turned"), 2 * k + 2)
                dve.tensor_copy(xT[:, k, NP:T], PS[:, (2 * k + 1) % 4, 0:P]).then_inc(sem("x_evac_dve"), 1)
                dve.wait_ge(sem("x_evac_dve"), k + 1)
                dve.wait_ge(sem("x_evac_act"), k + 1)
                add_square(xT[:, k, :])
            dve.sem_inc(sem("squares_summed"), 1)
            dve.wait_ge(sem("g_turned"), 1)
            dve.tensor_copy(gT[:, 0:65], PS[:, 7, 0:65]).then_inc(step, 1)
            dve.wait_ge(step, count.next())
            dve.tensor_scalar(gsub, GSUB, 1.0 - LAM_INIT, None, ALU.mult).then_inc(step, 1)
            count.next()
            dve.wait_ge(sem("lam_exps"), 1)
            dve.tensor_tensor(small[:, 8:9], small[:, 5:6], small[:, 4:5], ALU.subtract).then_inc(step, 1)
            dve.wait_ge(step, count.next())
            dve.tensor_scalar(neg_lam, small[:, 8:9], -LAM_INIT, None, ALU.add).then_inc(step, 1)
            dve.wait_ge(step, count.next())
            dve.scalar_tensor_tensor(out=comp, in0=cst[:, COMP1:COMP1 + 1], scalar=neg_lam, in1=cst[:, COMP0:COMP0 + 1],
                                     op0=ALU.mult, op1=ALU.add).then_inc(step, 1)
            dve.wait_ge(step, count.next())
            norm(0, 0, 0)
            ffn(0, BASE["ffn0"])
            norm(1, 1, 1)
            rows_out(nat[:, 0], BASE["qkv"], 0, 2)
            dve.wait_ge(sem("rows_read"), 3 * TB)
            rope(nat[:, 0])
            rows_out(nat[:, 1], BASE["qkv"], 2, 2)
            dve.wait_ge(sem("rows_read"), 5 * TB)
            dve.wait_ge(sem("rope_done"), 1)
            rope(nat[:, 1])
            rows_out(vN, BASE["qkv"], 4, 2)
            heads("A", 2)
            attend("A")
            dve.wait_ge(sem("o_readA"), primed(PAIR))
            dve.wait_ge(sem("oT_readA"), primed(2 * DB))

            def square_outputs(i):
                for u in range(2):
                    o = oT[:, i * 2 + u, :]
                    dve.tensor_tensor((sqacc, t2)[u][:, :], o, o, ALU.mult).then_inc(sem("o_squared"), 1)

            def scale_outputs(i, following):
                for u in range(2):
                    h = i * 2 + u
                    dve.wait_ge(sem("o_root"), h + 1)
                    dve.scalar_tensor_tensor(out=oT[:, h, :], in0=oT[:, h, :], scalar=gsub, in1=(t0, t1)[u][:, :],
                                             op0=ALU.mult, op1=ALU.mult).then_inc(sem("o_scaled"), 1)
                if following:
                    square_outputs(i + 1)
                for u in range(2):
                    h = i * 2 + u
                    dve.wait_ge(sem("oA_hi"), h + 1)
                    dve.tensor_tensor(xn_lo[:, h, :], oT[:, h, :], xn_hi[:, h, :].bitcast(F32), ALU.subtract).then_inc(
                        sem("oA_split"), 1)

            square_outputs(0)
            with dve.Fori(0, PAIR // 2 - 1) as i:
                scale_outputs(i, True)
            scale_outputs(PAIR // 2 - 1, False)
            add_down(BASE["oa"], 1.0, True)
            norm(2, 2, 2)
            ffn(1, BASE["ffn1"])
            norm(3, 3, G_KV)
            rows_out(nat[:, 0], BASE["kv"], 0, 2)
            dve.wait_ge(sem("av_stored"), 32)
            rows_out(vN, BASE["kv"], 2, 2)
            dve.wait_ge(w_used, BASE["wf"] + 1)
            zt = lfT
            dve.tensor_scalar(halves(zt), pair(3)[0:HB], small[0:HB, 3:4], None, ALU.add).then_inc(step, 1)
            dve.wait_ge(step, count.next())
            dve.scalar_tensor_tensor(out=lf1, in0=zt, scalar=-1.0, in1=zt, op0=ALU.mult, op1=ALU.max).then_inc(
                sem("absz_ready"), 1)
            heads("B", 1)
            dve.wait_ge(sem("LT_ready"), 1)
            dve.tensor_copy(LT, PS[:, 1, :]).then_inc(step, 1)
            count.next()
            dve.wait_ge(sem("ln_ready"), 1)
            dve.scalar_tensor_tensor(out=lfT, in0=zt, scalar=0.0, in1=lf1, op0=ALU.min, op1=ALU.subtract).then_inc(
                sem("logf_done"), 1)
            dve.wait_ge(sem("logf_done"), 1)
            ones16 = lf2[:, 0:NP]
            dve.memset(ones16, 1.0).then_inc(step, 1)
            dve.wait_ge(step, count.next())
            dve.tensor_tensor_scan(FCp, ones16, lfT[:, 0:NP], 0.0, ALU.mult, ALU.add).then_inc(step, 1)
            dve.memset(sqacc[:, 0:NP], 1.0).then_inc(step, 1)
            count.next()
            dve.wait_ge(step, count.next())
            dve.tensor_scalar(FCp, FCp, -1.0 / SCALE, None, ALU.mult).then_inc(step, 1)
            dve.tensor_tensor_scan(FC[:, 0:PAST], sqacc[:, 0:PAST], LT, 0.0, ALU.mult, ALU.add).then_inc(step, 1)
            count.next()
            count.next()
            dve.wait_ge(sem("lfN_ready"), 1)
            dve.tensor_copy(lfN, PS[:, 2, 0:TB * HB].rearrange("p (t h) -> p t h", t=TB)).then_inc(sem("lfN_read"), 1)
            dve.wait_ge(sem("lfN_read"), 1)
            same = cst[:, SAME:SAME + P].rearrange("p (b h) -> p b h", b=DB)
            new = lfN[:, TB - 1:TB, :].to_broadcast([P, DB, HB])
            dve.tensor_tensor(EX.rearrange("p (b h) -> p b h", b=DB), same, new, ALU.mult).then_inc(sem("EX_done"), 1)
            dve.wait_ge(sem("new_ready"), 1)
            dve.tensor_copy(small[:, 16:32], PS[:, 3, 0:DS]).then_inc(sem("new_read"), 1)
            dve.wait_ge(sem("new_read"), 1)
            dve.wait_ge(step, count.off + count.n)
            dve.tensor_tensor_scan(FC[:, PAST:PAST + DS], sqacc[:, 0:DS], small[:, 16:32], FC[:, PAST - 1:PAST], ALU.mult,
                                   ALU.add).then_inc(step, 1)
            dve.wait_ge(step, count.next())
            dve.tensor_scalar(LO[:, 0:PAST], FC[:, 0:PAST], -1.0 / SCALE, None, ALU.mult)
            mine = FC[:, PAST:PAST + DS].rearrange("p (o t) -> p o t", o=1).to_broadcast([P, DB, DS])
            dve.tensor_tensor(EX.rearrange("p (b h) -> p b h", b=DB), same, mine, ALU.mult).then_inc(step, 1)
            dve.wait_ge(step, count.next())
            dve.scalar_tensor_tensor(out=LO[:, PAST:T], in0=EX, scalar=-1.0 / SCALE, in1=cst[:, OTHER:OTHER + P],
                                     op0=ALU.mult, op1=ALU.add).then_inc(sem("LO_ready"), 1)
            norm(None, 4, 3)
            dve.wait_ge(sem("bk_stored"), 32)
            dve.wait_ge(sem("bf_stored"), 64)
            ffn(2, BASE["ffn2"])
            norm(4, 5, 4)
            with dve.Fori(0, KB // 2) as m:
                for u in range(2):
                    dve.wait_ge(w_used, BASE["qb"] + 1 + m * 2 + u)
                    dve.tensor_copy(halves(qraw[:, m * 2 + u, :]), pair(2 + u)).then_inc(sem("down_read"), 1)
            sums[0] += KB
            dve.wait_ge(sem("down_read"), sums[0] + 2)
            dve.tensor_copy(qT[:, :, :], qraw).then_inc(sem("qT_copied"), 1)
            attend("B")
            with dve.Fori(0, PAIR) as h:
                dve.wait_ge(sem("oB_hi"), h + 1)
                dve.tensor_tensor(xn_lo[:, h, :], oT[:, h, :], xn_hi[:, h, :].bitcast(F32), ALU.subtract).then_inc(
                    sem("oB_split"), 1)
            add_down(BASE["ob"], 1.0, True)
            norm(5, 6, 5)
            ffn(3, BASE["ffn3"])
            dve.wait_ge(sem("root_ready"), 6 + 1)
            for k in range(KB):
                dve.scalar_tensor_tensor(out=yT[:, k, :], in0=xT[:, k, :], scalar=gcol(G_FINAL, k), in1=t1[:, :],
                                         op0=ALU.mult, op1=ALU.mult).then_inc(sem("y_ready"), 1)
            for k in range(KB):
                dve.wait_ge(sem("y_turned"), 2 * k + 2)
                dve.tensor_copy(yN[:, 4, k * P:(k + 1) * P], PS[:, 4 + (2 * k + 1) % 4, 0:P]).then_inc(sem("y_evac_dve"), 1)


_INS = ['x_prompt', 'x_sample', 'cache_a_k', 'cache_a_v', 'cache_b_k', 'cache_b_v', 'cache_b_logf', 'g_norm', 'w_ffn_gate',
        'w_ffn_up', 'w_ffn_down', 'w_qkv_a', 'lambda_a', 'g_sub_a', 'w_o_a', 'g_kv_b', 'w_kv_b', 'w_f_b', 'b_f_b', 'w_q_b',
        'w_o_b', 'g_final']
_OUTS = [(1, NP, D), (DB, DS, D), (1, 1, NP, 8, 2, 64), (1, 1, NP, 8, 128), (1, NP, HB, 64), (1, NP, HB, 64), (1, NP, HB),
         (1, DB, DS, 8, 2, 64), (1, DB, DS, 8, 128), (DB, DS, HB, 64), (DB, DS, HB, 64), (DB, DS, HB)]


def shape_constants():
    import numpy as np
    p, j = np.arange(P)[:, None], np.arange(P)[None, :]
    c = np.zeros((P, NCONST), np.float32)
    c[:, IDENT:IDENT + P] = p == j
    c[:, CAUSAL:CAUSAL + P] = np.where(j > p, NEG, 0)
    c[:, CHUNKED:CHUNKED + P] = np.where((p < 64) & (j >= 64), NEG, 0)
    c[:, SPREAD:SPREAD + P] = (p // 32 == j // 32) & (p % 16 == j % 32)
    c[:, SAME:SAME + P] = p // 16 == j // 16
    c[:, OTHER:OTHER + P] = np.where(p // 16 == j // 16, 0, NEG)
    c[:, STEP:STEP + P] = p % 16 == j
    c[:, QSEL:QSEL + P] = p == j % 16
    c[:, QTRI:QTRI + P] = np.where(j % 16 > p, NEG, 0)
    c[:, COMP0] = (p[:, 0] // 16) % 2 == 0
    c[:, COMP1] = (p[:, 0] // 16) % 2 == 1
    inv = np.power(np.float32(500000.0), -np.arange(8, dtype=np.float32) * np.float32(2.0) / np.float32(16)).astype(np.float32)
    for t in range(TB):
        pos = (np.arange(P) + t * P if t < TB - 1 else PAST + np.arange(P) % DS).astype(np.float32)
        ang = (pos[:, None] * inv[None, :]).astype(np.float32).astype(np.float64)
        c[:, ROPE + 16 * t:ROPE + 16 * t + 8] = np.cos(ang)
        c[:, ROPE + 16 * t + 8:ROPE + 16 * t + 16] = np.sin(ang)
    own = np.where(np.arange(P)[None, :] // DS == np.arange(DB)[:, None], 0, NEG).astype(np.float32)
    return c, own.reshape(1, DB * P)


def kernel(**inputs):
    import numpy as _np
    import concourse.bacc as _bacc
    from concourse import mybir as _mybir
    from concourse.bass_utils import run_bass_kernel_spmd as _run

    nc = _bacc.Bacc("TRN2", target_bir_lowering=False, num_devices=1)
    arrays, args = {}, []
    consts = dict(zip(("shape_consts", "new_mask"), shape_constants()))
    for name in [*_INS, *consts]:
        a = _np.ascontiguousarray(inputs[name] if name in inputs else consts[name])
        arrays[f"in_{name}_dram"] = a
        args.append(nc.dram_tensor(f"in_{name}_dram", a.shape, _mybir.dt.from_np(a.dtype), kind="ExternalInput").ap())
    for i, shape in enumerate(_OUTS):
        args.append(nc.dram_tensor(f"out_{i}_dram", shape, F32, kind="ExternalOutput").ap())
    args.append(nc.dram_tensor("f_prompt_scr", (HB, NP), F32, kind="Internal").ap())
    args.append(nc.dram_tensor("f_sample_scr", (P, T), F32, kind="Internal").ap())
    yoco_stream_step(nc, *args)
    r = _run(nc, [arrays], core_ids=[0])
    return tuple(r.results[0][f"out_{i}_dram"] for i in range(len(_OUTS)))
```
